# Optimizing a Trainium2 kernel written in Bass

```python
import jax, jax.numpy as jnp
from jax import lax
import numpy as np
import math

D_MODEL = 1024
BATCH = 1
SEQ = 256
DEPTH = 2

GRID_W = 64
CTX_LEN = 256
N_EVEN = (DEPTH + 1) // 2
N_ODD = DEPTH // 2
EPS = 1e-6
A_CH = D_MODEL // 2
CONV_K = 31
B_CH = D_MODEL // 2
B_HEADS = 8
B_HD = B_CH // B_HEADS
CHUNK = 128
IN_E = 2 * A_CH + 2 * B_CH
QK_NOPE = 128
QK_ROPE = 64
V_HD = 128
MLA_HEADS = D_MODEL // V_HD
Q_RANK = 384
KV_RANK = 256
IN_O = Q_RANK + KV_RANK + QK_ROPE
ROPE_AXIS = QK_ROPE // 2
ROPE_FREQS = ROPE_AXIS // 2
ROPE_BASE = 10000.0
Q_BLOCK = 128
ATTN_SCALE = (QK_NOPE + QK_ROPE) ** -0.5
D_FF = 2816
N_EXPERTS = 8
TOP_K = 2
D_EXPERT = 3584


def _rmsnorm(x, g):
    xf = x.astype(jnp.float32)
    y = xf * lax.rsqrt(jnp.mean(xf * xf, axis=-1, keepdims=True) + EPS)
    return (y * g.astype(jnp.float32)).astype(x.dtype)

def _layernorm(x, g, b):
    xf = x.astype(jnp.float32)
    mu = jnp.mean(xf, axis=-1, keepdims=True)
    var = jnp.mean(jnp.square(xf - mu), axis=-1, keepdims=True)
    y = (xf - mu) * lax.rsqrt(var + EPS)
    return (y * g.astype(jnp.float32) + b.astype(jnp.float32)).astype(x.dtype)

def _modulate(h, shift, scale):
    return h * (1 + scale[:, None, :]) + shift[:, None, :]

def _swiglu(h, w1, w3, w2):
    return (jax.nn.silu(h @ w1) * (h @ w3)) @ w2

def _rope2d(x, cos, sin):
    xs = x.reshape(*x.shape[:-1], 2, 2, ROPE_FREQS)
    x1, x2 = xs[..., 0, :], xs[..., 1, :]
    c = cos[None, :, None].astype(x.dtype)
    s = sin[None, :, None].astype(x.dtype)
    out = jnp.stack([x1 * c - x2 * s, x1 * s + x2 * c], axis=-2)
    return out.reshape(x.shape)

def _conv_gmlp_mixer(h, w_in, conv_w, conv_b, ln_a_g, ln_a_b, ln_v_g, ln_v_b, w_s, b_s, w_out):
    b, t, _ = h.shape
    z = h @ w_in
    a_val, a_gate, u, v = jnp.split(z, 4, axis=-1)
    a = a_val * jax.nn.sigmoid(a_gate)
    a = lax.conv_general_dilated(
        a, conv_w.reshape(CONV_K, 1, A_CH).astype(a.dtype), window_strides=(1,),
        padding=[(CONV_K // 2, CONV_K // 2)], dimension_numbers=('NWC', 'WIO', 'NWC'),
        feature_group_count=A_CH) + conv_b
    a = jax.nn.silu(_layernorm(a, ln_a_g, ln_a_b))
    u = jax.nn.gelu(u)
    v = _layernorm(jax.nn.gelu(v), ln_v_g, ln_v_b).reshape(b, t // CHUNK, CHUNK, B_HEADS, B_HD)
    sv = jnp.einsum('hij,bnjhd->bnihd', w_s, v) + b_s.T[None, None, :, :, None]
    bo = u * sv.reshape(b, t, B_CH)
    return jnp.concatenate([a, bo], axis=-1) @ w_out

def _mla_q(q_lat, g_q, w_uq, rope):
    b, t, _ = q_lat.shape
    q = (_rmsnorm(q_lat, g_q) @ w_uq).reshape(b, t, MLA_HEADS, QK_NOPE + QK_ROPE)
    if rope is not None:
        q = jnp.concatenate([q[..., :QK_NOPE], _rope2d(q[..., QK_NOPE:], *rope)], axis=-1)
    return q

def _mla_kv(kv_lat, k_pe, g_kv, w_ukv, rope):
    b, t, _ = kv_lat.shape
    kv = (_rmsnorm(kv_lat, g_kv) @ w_ukv).reshape(b, t, MLA_HEADS, QK_NOPE + V_HD)
    k_pe = k_pe[:, :, None, :]
    if rope is not None:
        k_pe = _rope2d(k_pe, *rope)
    k = jnp.concatenate([kv[..., :QK_NOPE], jnp.broadcast_to(k_pe, (b, t, MLA_HEADS, QK_ROPE))], axis=-1)
    return k, kv[..., QK_NOPE:]

def _attend(q, k, v):
    b, tq, h, dq = q.shape
    nb = tq // Q_BLOCK
    qb = jnp.moveaxis(q.reshape(b, nb, Q_BLOCK, h, dq), 1, 0)

    def block(qblk):
        s = jnp.einsum('bqhd,bkhd->bhqk', qblk, k).astype(jnp.float32) * ATTN_SCALE
        p = jax.nn.softmax(s, axis=-1).astype(v.dtype)
        return jnp.einsum('bhqk,bkhd->bqhd', p, v)

    o = lax.map(block, qb)
    return jnp.moveaxis(o, 0, 1).reshape(b, tq, h * v.shape[-1])

def _moe(h, router, w1, w3, w2):
    b, t, d = h.shape
    hf = h.reshape(b * t, d)
    logits = (hf @ router).astype(jnp.float32)
    top_v, top_i = lax.top_k(logits, TOP_K)
    top_w = jax.nn.softmax(top_v, axis=-1)
    gates = jnp.sum(jax.nn.one_hot(top_i, N_EXPERTS, dtype=jnp.float32) * top_w[..., None], axis=-2).astype(h.dtype)
    y = jnp.zeros_like(hf)
    for e in range(N_EXPERTS):
        y = y + gates[:, e:e + 1] * _swiglu(hf, w1[e], w3[e], w2[e])
    return y.reshape(b, t, d)

def first_inputs(seed: int = 0) -> dict:
    key = jax.random.key(seed)
    ks = iter(jax.random.split(key, 64))

    def nrm(shape, s=1.0):
        return jax.random.normal(next(ks), shape, jnp.float32) * s

    def gain(shape):
        return 1.0 + nrm(shape, 0.02)

    D = D_MODEL
    return {
        'x': nrm((BATCH, SEQ, D)),
        'c': nrm((BATCH, D)),
        'ctx': nrm((BATCH, CTX_LEN, D)),
        'c_ctx': nrm((D,)),
        'w_ada': nrm((DEPTH, D, 6 * D), 0.5 * D ** -0.5),
        'b_ada': nrm((DEPTH, 6 * D), 0.02),
        'norm_g': gain((DEPTH, 2, D)),
        'e_w_in': nrm((N_EVEN, D, IN_E), D ** -0.5),
        'e_conv_w': nrm((N_EVEN, CONV_K, A_CH), CONV_K ** -0.5),
        'e_conv_b': nrm((N_EVEN, A_CH), 0.02),
        'e_ln_a_g': gain((N_EVEN, A_CH)),
        'e_ln_a_b': nrm((N_EVEN, A_CH), 0.02),
        'e_ln_v_g': gain((N_EVEN, B_CH)),
        'e_ln_v_b': nrm((N_EVEN, B_CH), 0.02),
        'e_w_s': nrm((N_EVEN, B_HEADS, CHUNK, CHUNK), CHUNK ** -0.5),
        'e_b_s': gain((N_EVEN, B_HEADS, CHUNK)),
        'e_w_out': nrm((N_EVEN, A_CH + B_CH, D), (A_CH + B_CH) ** -0.5),
        'e_ffn_w1': nrm((N_EVEN, D, D_FF), D ** -0.5),
        'e_ffn_w3': nrm((N_EVEN, D, D_FF), D ** -0.5),
        'e_ffn_w2': nrm((N_EVEN, D_FF, D), D_FF ** -0.5),
        'o_w_in': nrm((N_ODD, D, IN_O), D ** -0.5),
        'o_g_q': gain((N_ODD, Q_RANK)),
        'o_g_kv': gain((N_ODD, KV_RANK)),
        'o_w_uq': nrm((N_ODD, Q_RANK, MLA_HEADS * (QK_NOPE + QK_ROPE)), Q_RANK ** -0.5),
        'o_w_ukv': nrm((N_ODD, KV_RANK, MLA_HEADS * (QK_NOPE + V_HD)), KV_RANK ** -0.5),
        'o_w_o': nrm((N_ODD, MLA_HEADS * V_HD, D), (MLA_HEADS * V_HD) ** -0.5),
        'o_router': nrm((N_ODD, D, N_EXPERTS), D ** -0.5),
        'o_exp_w1': nrm((N_ODD, N_EXPERTS, D, D_EXPERT), D ** -0.5),
        'o_exp_w3': nrm((N_ODD, N_EXPERTS, D, D_EXPERT), D ** -0.5),
        'o_exp_w2': nrm((N_ODD, N_EXPERTS, D_EXPERT, D), D_EXPERT ** -0.5),
        'final_g': gain((D,)),
    }

def first_block(x, c, ctx, c_ctx, w_ada, b_ada, norm_g,
              e_w_in, e_conv_w, e_conv_b, e_ln_a_g, e_ln_a_b, e_ln_v_g, e_ln_v_b,
              e_w_s, e_b_s, e_w_out, e_ffn_w1, e_ffn_w3, e_ffn_w2,
              o_w_in, o_g_q, o_g_kv, o_w_uq, o_w_ukv, o_w_o,
              o_router, o_exp_w1, o_exp_w3, o_exp_w2, final_g):
    b, t, _ = x.shape
    rows = t // GRID_W
    row = jnp.repeat(jnp.arange(rows), GRID_W).astype(jnp.float32)
    col = jnp.tile(jnp.arange(GRID_W), rows).astype(jnp.float32)
    inv_freq = ROPE_BASE ** (-jnp.arange(ROPE_FREQS, dtype=jnp.float32) / ROPE_FREQS)
    ang = jnp.stack([row[:, None] * inv_freq, col[:, None] * inv_freq], axis=1)
    rope = (jnp.cos(ang), jnp.sin(ang))

    silu_c = jax.nn.silu(c)
    silu_cc = jax.nn.silu(c_ctx)[None]

    for i in range(DEPTH):
        last = i == DEPTH - 1
        j = i // 2
        mx = jnp.split(silu_c @ w_ada[i] + b_ada[i], 6, axis=-1)
        mc = jnp.split(silu_cc @ w_ada[i] + b_ada[i], 6, axis=-1)
        hx = _modulate(_rmsnorm(x, norm_g[i, 0]), mx[0], mx[1])
        hc = _modulate(_rmsnorm(ctx, norm_g[i, 0]), mc[0], mc[1])

        if i % 2 == 0:
            params = (e_w_in[j], e_conv_w[j], e_conv_b[j], e_ln_a_g[j], e_ln_a_b[j],
                      e_ln_v_g[j], e_ln_v_b[j], e_w_s[j], e_b_s[j], e_w_out[j])
            x = x + mx[2][:, None] * _conv_gmlp_mixer(hx, *params)
            if not last:
                ctx = ctx + mc[2][:, None] * _conv_gmlp_mixer(hc, *params)
        else:
            zx = hx @ o_w_in[j]
            q_lat_x, kv_lat_x, kpe_x = jnp.split(zx, [Q_RANK, Q_RANK + KV_RANK], axis=-1)
            if last:
                zc = hc @ o_w_in[j][:, Q_RANK:]
                kv_lat_c, kpe_c = jnp.split(zc, [KV_RANK], axis=-1)
            else:
                zc = hc @ o_w_in[j]
                q_lat_c, kv_lat_c, kpe_c = jnp.split(zc, [Q_RANK, Q_RANK + KV_RANK], axis=-1)
            k_c, v_c = _mla_kv(kv_lat_c, kpe_c, o_g_kv[j], o_w_ukv[j], None)
            k_x, v_x = _mla_kv(kv_lat_x, kpe_x, o_g_kv[j], o_w_ukv[j], rope)
            q_x = _mla_q(q_lat_x, o_g_q[j], o_w_uq[j], rope)
            att_x = _attend(q_x, jnp.concatenate([k_c, k_x], axis=1), jnp.concatenate([v_c, v_x], axis=1))
            x = x + mx[2][:, None] * (att_x @ o_w_o[j])
            if not last:
                q_c = _mla_q(q_lat_c, o_g_q[j], o_w_uq[j], None)
                att_c = _attend(q_c, k_c, v_c)
                ctx = ctx + mc[2][:, None] * (att_c @ o_w_o[j])

        if i % 2 == 0:
            ffn = lambda h: _swiglu(h, e_ffn_w1[j], e_ffn_w3[j], e_ffn_w2[j])
        else:
            ffn = lambda h: _moe(h, o_router[j], o_exp_w1[j], o_exp_w3[j], o_exp_w2[j])
        hx = _modulate(_rmsnorm(x, norm_g[i, 1]), mx[3], mx[4])
        x = x + mx[5][:, None] * ffn(hx)
        if not last:
            hc = _modulate(_rmsnorm(ctx, norm_g[i, 1]), mc[3], mc[4])
            ctx = ctx + mc[5][:, None] * ffn(hc)

    return _rmsnorm(x, final_g)


DEPTH_2 = 1

HEAD_DIM = 64
ATTN_SCALE_2 = HEAD_DIM ** -0.5
SWA_HEADS = 8
SWA_KV_HEADS = 2
SWA_WINDOW = 128
SWA_Q = SWA_HEADS * HEAD_DIM
SWA_KV = SWA_KV_HEADS * HEAD_DIM
SSM_WIDTH = 512
SSM_GROUP = 16
SSM_GROUPS = SSM_WIDTH // SSM_GROUP
SSM_STATE = 64
DT_MIN = 0.001
DT_MAX = 0.1
MOBA_HEADS = 8
MOBA_KV_HEADS = 2
MOBA_BLOCK = 256
MOBA_TOPK = 3
MOBA_Q_CHUNK = 64
MOBA_Q = MOBA_HEADS * HEAD_DIM
MOBA_KV = MOBA_KV_HEADS * HEAD_DIM
N_BRANCH = 3
D_FF_2 = 4 * D_MODEL
NORM_EPS = 1e-6
ALIBI_MAX_BIAS = 8.0
IN_SIZES = (SWA_Q, SWA_KV, SWA_KV, SSM_WIDTH, MOBA_Q, MOBA_KV, MOBA_KV, N_BRANCH * D_MODEL)
D_IN = sum(IN_SIZES)


def rms_norm(x, gain):
    xf = x.astype(jnp.float32)
    y = xf * lax.rsqrt(jnp.mean(xf * xf, axis=-1, keepdims=True) + NORM_EPS)
    return (y * gain.astype(jnp.float32)).astype(x.dtype)

def alibi_slopes():
    n = SWA_HEADS + MOBA_HEADS
    return jnp.asarray(2.0 ** (-ALIBI_MAX_BIAS * np.arange(1, n + 1) / n), jnp.float32)

def split_in(proj):
    outs, start = [], 0
    for size in IN_SIZES:
        outs.append(proj[..., start:start + size])
        start += size
    return outs

def swa_attention(q, k, v, sinks, slopes):
    B, S, Hq, d = q.shape
    Hkv = k.shape[2]
    G = Hq // Hkv
    W = SWA_WINDOW
    nb = S // W
    qb = q.reshape(B, nb, W, Hkv, G, d)
    kp = jnp.pad(k, ((0, 0), (W, 0), (0, 0), (0, 0))).reshape(B, nb + 1, W, Hkv, d)
    vp = jnp.pad(v, ((0, 0), (W, 0), (0, 0), (0, 0))).reshape(B, nb + 1, W, Hkv, d)
    kb = jnp.concatenate([kp[:, :-1], kp[:, 1:]], axis=2)
    vb = jnp.concatenate([vp[:, :-1], vp[:, 1:]], axis=2)
    s = jnp.einsum('bnqhgd,bnkhd->bnhgqk', qb, kb).astype(jnp.float32) * ATTN_SCALE_2
    t_rel = jnp.arange(W)[:, None]
    s_rel = jnp.arange(2 * W)[None, :] - W
    dist = t_rel - s_rel
    band = (dist >= 0) & (dist < W)
    mask = band[None] & ((jnp.arange(nb)[:, None, None] * W + s_rel[None]) >= 0)
    bias = -slopes.reshape(Hkv, G)[:, :, None, None] * dist.astype(jnp.float32)[None, None]
    s = jnp.where(mask[None, :, None, None], s + bias[None, None], -jnp.inf)
    sink = jnp.broadcast_to(sinks.astype(jnp.float32).reshape(Hkv, G)[None, None, :, :, None, None],
                            s.shape[:-1] + (1,))
    p = jax.nn.softmax(jnp.concatenate([s, sink], axis=-1), axis=-1)[..., :-1].astype(v.dtype)
    o = jnp.einsum('bnhgqk,bnkhd->bnqhgd', p, vb)
    return o.reshape(B, S, Hq * d)

def moba_attention(q, k, v, slopes):
    B, S, Hq, d = q.shape
    Hkv = k.shape[2]
    G = Hq // Hkv
    L = MOBA_BLOCK
    Qc = MOBA_Q_CHUNK
    Sp = -(-S // L) * L
    nblk = Sp // L
    topk = min(MOBA_TOPK, nblk)
    pad = ((0, 0), (0, Sp - S), (0, 0), (0, 0))
    q, k, v = jnp.pad(q, pad), jnp.pad(k, pad), jnp.pad(v, pad)
    k_blocks = jnp.repeat(k, G, axis=2).transpose(0, 2, 1, 3).reshape(B, Hq, nblk, L, d)
    v_blocks = jnp.repeat(v, G, axis=2).transpose(0, 2, 1, 3).reshape(B, Hq, nblk, L, d)
    k_mean = jnp.mean(k_blocks.astype(jnp.float32), axis=3)
    nq = Sp // Qc
    q_chunks = q.transpose(0, 2, 1, 3).reshape(B, Hq, nq, Qc, d).transpose(2, 0, 1, 3, 4)
    b_idx = jnp.arange(B)[:, None, None, None]
    h_idx = jnp.arange(Hq)[None, :, None, None]
    blk_ids = jnp.arange(nblk)
    rank_ids = jnp.arange(topk)
    offs = jnp.arange(L)

    def one_chunk(args):
        qi, ci = args
        t = ci * Qc + jnp.arange(Qc)
        j = (ci * Qc) // L
        gate = jnp.einsum('bhqd,bhnd->bhqn', qi.astype(jnp.float32), k_mean)
        gate = jnp.where(blk_ids < j, gate, -jnp.inf)
        _, sel = lax.top_k(gate, topk)
        valid = rank_ids < j
        k_sel = k_blocks[b_idx, h_idx, sel]
        v_sel = v_blocks[b_idx, h_idx, sel]
        s_sel = jnp.einsum('bhqd,bhqrkd->bhqrk', qi, k_sel).astype(jnp.float32) * ATTN_SCALE_2
        dist_sel = (t[None, None, :, None, None] - (sel[..., None] * L + offs)).astype(jnp.float32)
        s_sel = s_sel - slopes[None, :, None, None, None] * dist_sel
        s_sel = jnp.where(valid[None, None, None, :, None], s_sel, -jnp.inf)
        k_own = lax.dynamic_slice_in_dim(k_blocks, j, 1, axis=2)[:, :, 0]
        v_own = lax.dynamic_slice_in_dim(v_blocks, j, 1, axis=2)[:, :, 0]
        s_own = jnp.einsum('bhqd,bhkd->bhqk', qi, k_own).astype(jnp.float32) * ATTN_SCALE_2
        dist_own = t[:, None] - (j * L + offs)[None, :]
        s_own = s_own - slopes[None, :, None, None] * dist_own.astype(jnp.float32)[None, None]
        s_own = jnp.where((dist_own >= 0)[None, None], s_own, -jnp.inf)
        logits = jnp.concatenate([s_sel.reshape(B, Hq, Qc, topk * L), s_own], axis=-1)
        p = jax.nn.softmax(logits, axis=-1).astype(v_blocks.dtype)
        p_sel = p[..., :topk * L].reshape(B, Hq, Qc, topk, L)
        o = (jnp.einsum('bhqrk,bhqrkd->bhqd', p_sel, v_sel)
             + jnp.einsum('bhqk,bhkd->bhqd', p[..., topk * L:], v_own))
        return o

    o = lax.map(one_chunk, (q_chunks, jnp.arange(nq)))
    o = o.transpose(1, 0, 3, 2, 4).reshape(B, Sp, Hq * d)
    return o[:, :S]

def s5_ssm(u, lam_re, lam_im, log_step, b_re, b_im, c_re, c_im, d_skip):
    Bsz, S, _ = u.shape
    f32 = jnp.float32
    uf = u.astype(f32).reshape(Bsz, S, SSM_GROUPS, SSM_GROUP)
    lr, li = lam_re.astype(f32), lam_im.astype(f32)
    dt = jnp.exp(log_step.astype(f32))[:, None]
    mag = jnp.exp(lr * dt)
    ab_re, ab_im = mag * jnp.cos(li * dt), mag * jnp.sin(li * dt)
    den = lr * lr + li * li
    nr, ni = ab_re - 1.0, ab_im
    f_re, f_im = (nr * lr + ni * li) / den, (ni * lr - nr * li) / den
    br, bi = b_re.astype(f32), b_im.astype(f32)
    bb_re = f_re[..., None] * br - f_im[..., None] * bi
    bb_im = f_re[..., None] * bi + f_im[..., None] * br
    x_re = jnp.einsum('bsgh,gph->bsgp', uf, bb_re)
    x_im = jnp.einsum('bsgh,gph->bsgp', uf, bb_im)
    a_re = jnp.broadcast_to(ab_re, x_re.shape)
    a_im = jnp.broadcast_to(ab_im, x_im.shape)

    def combine(e1, e2):
        a1r, a1i, b1r, b1i = e1
        a2r, a2i, b2r, b2i = e2
        return (a2r * a1r - a2i * a1i, a2r * a1i + a2i * a1r,
                a2r * b1r - a2i * b1i + b2r, a2r * b1i + a2i * b1r + b2i)

    _, _, h_re, h_im = lax.associative_scan(combine, (a_re, a_im, x_re, x_im), axis=1)
    y = (jnp.einsum('bsgp,ghp->bsgh', h_re, c_re.astype(f32))
         - jnp.einsum('bsgp,ghp->bsgh', h_im, c_im.astype(f32))
         + d_skip.astype(f32).reshape(SSM_GROUPS, SSM_GROUP) * uf)
    return y.reshape(Bsz, S, SSM_WIDTH)

def second_inputs(seed: int = 0) -> dict:
    key = jax.random.key(seed)
    ks = jax.random.split(key, 24)
    f32 = jnp.float32
    nrm = lambda k, shape, scale: jax.random.normal(k, shape, f32) * scale
    x = jax.random.normal(ks[0], (BATCH, SEQ, D_MODEL), f32)
    norm_mix = 1.0 + nrm(ks[1], (DEPTH_2, D_MODEL), 0.02)
    w_in = nrm(ks[2], (DEPTH_2, D_MODEL, D_IN), D_MODEL ** -0.5)
    sinks = nrm(ks[3], (DEPTH_2, SWA_HEADS), 0.5)
    lam_re = -0.5 + nrm(ks[4], (DEPTH_2, SSM_GROUPS, SSM_STATE), 0.01)
    lam_im = (math.pi * jnp.arange(SSM_STATE, dtype=f32))[None, None, :] + nrm(ks[5], (DEPTH_2, SSM_GROUPS, SSM_STATE), 0.01)
    log_step = math.log(DT_MIN) + jax.random.uniform(ks[6], (DEPTH_2, SSM_GROUPS), f32) * (math.log(DT_MAX) - math.log(DT_MIN))
    b_re = nrm(ks[7], (DEPTH_2, SSM_GROUPS, SSM_STATE, SSM_GROUP), (2 * SSM_GROUP) ** -0.5)
    b_im = nrm(ks[8], (DEPTH_2, SSM_GROUPS, SSM_STATE, SSM_GROUP), (2 * SSM_GROUP) ** -0.5)
    c_re = nrm(ks[9], (DEPTH_2, SSM_GROUPS, SSM_GROUP, SSM_STATE), (2 * SSM_STATE) ** -0.5)
    c_im = nrm(ks[10], (DEPTH_2, SSM_GROUPS, SSM_GROUP, SSM_STATE), (2 * SSM_STATE) ** -0.5)
    d_skip = nrm(ks[11], (DEPTH_2, SSM_WIDTH), 1.0)
    w_glu = nrm(ks[12], (DEPTH_2, SSM_WIDTH, 2 * SSM_WIDTH), SSM_WIDTH ** -0.5)
    w_o_swa = nrm(ks[13], (DEPTH_2, SWA_Q, D_MODEL), SWA_Q ** -0.5)
    w_o_ssm = nrm(ks[14], (DEPTH_2, SSM_WIDTH, D_MODEL), SSM_WIDTH ** -0.5)
    w_o_moba = nrm(ks[15], (DEPTH_2, MOBA_Q, D_MODEL), MOBA_Q ** -0.5)
    w_out = nrm(ks[16], (DEPTH_2, D_MODEL, D_MODEL), D_MODEL ** -0.5)
    norm_ffn = 1.0 + nrm(ks[17], (DEPTH_2, D_MODEL), 0.02)
    w_ff1 = nrm(ks[18], (DEPTH_2, D_MODEL, D_FF_2), D_MODEL ** -0.5)
    w_ff2 = nrm(ks[19], (DEPTH_2, D_FF_2, D_MODEL), D_FF_2 ** -0.5)
    norm_final = 1.0 + nrm(ks[20], (D_MODEL,), 0.02)
    return {"x": x, "norm_mix": norm_mix, "w_in": w_in, "sinks": sinks,
            "lam_re": lam_re, "lam_im": lam_im, "log_step": log_step,
            "b_re": b_re, "b_im": b_im, "c_re": c_re, "c_im": c_im, "d_skip": d_skip,
            "w_glu": w_glu, "w_o_swa": w_o_swa, "w_o_ssm": w_o_ssm, "w_o_moba": w_o_moba,
            "w_out": w_out, "norm_ffn": norm_ffn, "w_ff1": w_ff1, "w_ff2": w_ff2,
            "norm_final": norm_final}

def second_block(x, norm_mix, w_in, sinks, lam_re, lam_im, log_step, b_re, b_im, c_re, c_im,
              d_skip, w_glu, w_o_swa, w_o_ssm, w_o_moba, w_out, norm_ffn, w_ff1, w_ff2,
              norm_final):
    B, S, _ = x.shape
    slopes = alibi_slopes()
    slopes_swa, slopes_moba = slopes[:SWA_HEADS], slopes[SWA_HEADS:]
    for l in range(DEPTH_2):
        h = rms_norm(x, norm_mix[l])
        qa, ka, va, u, qm, km, vm, gates = split_in(h @ w_in[l])
        oa = swa_attention(qa.reshape(B, S, SWA_HEADS, HEAD_DIM),
                           ka.reshape(B, S, SWA_KV_HEADS, HEAD_DIM),
                           va.reshape(B, S, SWA_KV_HEADS, HEAD_DIM), sinks[l], slopes_swa)
        ya = oa @ w_o_swa[l]
        ys = s5_ssm(u, lam_re[l], lam_im[l], log_step[l], b_re[l], b_im[l], c_re[l], c_im[l], d_skip[l])
        z = jax.nn.gelu(ys).astype(x.dtype) @ w_glu[l]
        yb = (z[..., :SSM_WIDTH] * jax.nn.sigmoid(z[..., SSM_WIDTH:])) @ w_o_ssm[l]
        om = moba_attention(qm.reshape(B, S, MOBA_HEADS, HEAD_DIM),
                            km.reshape(B, S, MOBA_KV_HEADS, HEAD_DIM),
                            vm.reshape(B, S, MOBA_KV_HEADS, HEAD_DIM), slopes_moba)
        yc = om @ w_o_moba[l]
        g = jax.nn.sigmoid(gates)
        mixed = (g[..., :D_MODEL] * ya + g[..., D_MODEL:2 * D_MODEL] * yb
                 + g[..., 2 * D_MODEL:] * yc)
        x = x + mixed @ w_out[l]
        h = rms_norm(x, norm_ffn[l])
        x = x + jnp.square(jax.nn.relu(h @ w_ff1[l])) @ w_ff2[l]
    return rms_norm(x, norm_final)


def setup_inputs(seed=0):
    out = dict(first_inputs(seed))
    for name, value in second_inputs(seed + 1).items():
        if name != "x":
            out[name + "_2"] = value
    return out


def reference(
    x, c, ctx, c_ctx, w_ada, b_ada, norm_g, e_w_in, e_conv_w, e_conv_b, e_ln_a_g, e_ln_a_b,
    e_ln_v_g, e_ln_v_b, e_w_s, e_b_s, e_w_out, e_ffn_w1, e_ffn_w3, e_ffn_w2, o_w_in, o_g_q,
    o_g_kv, o_w_uq, o_w_ukv, o_w_o, o_router, o_exp_w1, o_exp_w3, o_exp_w2, final_g, norm_mix_2,
    w_in_2, sinks_2, lam_re_2, lam_im_2, log_step_2, b_re_2, b_im_2, c_re_2, c_im_2, d_skip_2,
    w_glu_2, w_o_swa_2, w_o_ssm_2, w_o_moba_2, w_out_2, norm_ffn_2, w_ff1_2, w_ff2_2,
    norm_final_2,
):
    x = first_block(
        x, c, ctx, c_ctx, w_ada, b_ada, norm_g, e_w_in, e_conv_w, e_conv_b, e_ln_a_g, e_ln_a_b,
        e_ln_v_g, e_ln_v_b, e_w_s, e_b_s, e_w_out, e_ffn_w1, e_ffn_w3, e_ffn_w2, o_w_in, o_g_q,
        o_g_kv, o_w_uq, o_w_ukv, o_w_o, o_router, o_exp_w1, o_exp_w3, o_exp_w2, final_g,
    )
    return second_block(
        x, norm_mix_2, w_in_2, sinks_2, lam_re_2, lam_im_2, log_step_2, b_re_2, b_im_2, c_re_2,
        c_im_2, d_skip_2, w_glu_2, w_o_swa_2, w_o_ssm_2, w_o_moba_2, w_out_2, norm_ffn_2,
        w_ff1_2, w_ff2_2, norm_final_2,
    )


_drawn_inputs = setup_inputs


def setup_inputs(seed=0):
    import zlib

    import numpy as np

    out = dict(_drawn_inputs(seed))
    spreads = {}
    factors = {'e_conv_b': 8.0,
     'e_ln_a_g': 7.093,
     'e_ln_a_b': 7.167,
     'e_ln_v_g': 8.0,
     'e_ln_v_b': 8.0,
     'e_b_s': 8.0,
     'o_g_q': 8.0,
     'o_g_kv': 8.0,
     'norm_mix_2': 5.911,
     'sinks_2': 77.425,
     'lam_re_2': 64.0,
     'lam_im_2': 37.52,
     'log_step_2': 39.384,
     'b_re_2': 52.28,
     'b_im_2': 53.024,
     'c_re_2': 52.872,
     'c_im_2': 51.68,
     'norm_ffn_2': 8.721,
     'norm_final_2': 22.541}
    for name, (base, spread) in spreads.items():
        noise = np.random.default_rng([zlib.crc32(name.encode()), seed]).standard_normal(out[name].shape)
        drawn = base * np.exp(spread * noise) if base else spread * noise
        out[name] = __import__('jax').numpy.asarray(drawn.astype(out[name].dtype))
    for name, factor in factors.items():
        out[name] = (out[name] * factor).astype(out[name].dtype)
    return out
```

```python
from contextlib import ExitStack

import numpy as np

import concourse.bass as bass
from concourse import mybir

F32 = mybir.dt.float32
F32R = mybir.dt.float32r
I32 = mybir.dt.int32
ALU = mybir.AluOpType
ACT = mybir.ActivationFunctionType
AX = mybir.AxisListType.X

P = 128
D = 1024
T = 256
KT = D // P
DEPTH = 2
EPS = 1e-6
CONV_K = 31
PAD = CONV_K // 2
B_HEADS = 8
MLA_HEADS = 8
NOPE, ROPE, V_HD = 128, 64, 128
Q_RANK, KV_RANK = 384, 256
MLA_SCALE = (NOPE + ROPE) ** -0.5
D_FF = 2816
FT = D_FF // P
N_EXPERTS = 8
D_EXPERT = 3584
ET = D_EXPERT // P
SPARE = 2 * T // (P + 1)
N_ITEMS = N_EXPERTS + SPARE
HEAD = 64
SCALE2 = HEAD ** -0.5
N_HEADS2 = 16
SWA_WINDOW = 128
SSM_TILES = 16
SSM_L = 128
FF2 = 4096
SLOPES = 2.0 ** (-8.0 * np.arange(1, N_HEADS2 + 1) / N_HEADS2)

RING = 3
SLOT = 4096

CH_ADA0, CH_Z, CH_ADA1, CH_OUT0 = 0, 12, 16, 28
CH_UP, CH_DOWN, CH_KV, CH_Q, CH_UKV, CH_UQ, CH_WO = 30, 41, 47, 48, 49, 50, 52
N_FIRST = 54
TWO_PARTS = range(CH_UP, CH_DOWN)
UPS, DOWNS = D_EXPERT // 256, ET // 4
PER_EXPERT = UPS + DOWNS
ADA_BANKS = (0, 1, 3)
C2_A, C2_B, C2_QA, C2_QM, C2_GATE, C2_SWA, C2_MOBA, C2_GLU, C2_SSM, C2_OUT, C2_FF1, C2_FF2 = (
    0, 1, 2, 3, 4, 10, 11, 12, 13, 14, 16, 24)
N_SECOND = 32


def parts(n):
    return 2 if n in TWO_PARTS else 1


def landed(n):
    return 16 * sum(parts(m) for m in range(n % RING, n + 1, RING))


QUARTER, SPLIT = SLOT // 4, 4
QUARTERS, UP_QUARTERS = 4 * PER_EXPERT, 4 * UPS


def expert_landed(j):
    return 16 * sum(2 if m < UPS else 1 for m in range(j % RING, j + 1, RING))


FIRST_TOTAL = [landed(N_FIRST - RING + s) for s in range(RING)]
EXPERT_TOTAL = [expert_landed(PER_EXPERT - RING + s) for s in range(RING)]


def expert_chunk_ready(it, j):
    return FIRST_TOTAL[j % RING] + expert_landed(j) + it * EXPERT_TOTAL[j % RING]


REGION = 25600


def columns(sizes):
    at, out = 0, {}
    for name, n in sizes:
        out[name] = (at, at + n)
        at += n
    return out, at


CONST_COLS, N_CONST = columns([("ident", P), ("tri", P), ("iota", P), ("iota8", 8), ("swa_dist", 384),
                               ("moba_dist", 384), ("rot", ROPE), ("cos", T), ("sin", T)])
PARAM_COLS, N_PARAM = columns([("c", 16), ("norm_g", 32), ("b_ada", 96), ("final_g", 8), ("norm_mix", 8),
                               ("norm_ffn", 8), ("norm_final", 8), ("conv_b", 4), ("ln_a_g", 4),
                               ("ln_a_b", 4), ("d_skip", 4), ("g_q", 3), ("g_kv", 2), ("conv_w", 4 * CONV_K),
                               ("lam_re", 16), ("lam_im", 16), ("log_step", 16), ("sinks", 8),
                               ("router", KT * N_EXPERTS)])
FAR = 1e33

NORMS = [(KT, 2, True), (KT, 2, True), (KT, 2, True), (2, 2, False), (3, 1, False), (KT, 1, True),
         (KT, 1, False), (KT, 1, False), (KT, 1, False), (KT, 1, False)]
(N_MIX0, N_FFN0, N_MIX1, N_KV, N_Q, N_MOE, N_END1, N_MIX2, N_FFN2, N_END2) = range(10)


def tiles_before(n):
    return sum(kt for kt, _, _ in NORMS[:n])


def modulated_before(n):
    return sum(kt for kt, _, mod in NORMS[:n] if mod)


X_MIX0, X_FFN0, X_MIX1, X_MOE, X_MIX2, X_FFN2 = (KT * i for i in range(1, 7))

PROJ = ([(C2_A, "dup", 0, ("ka", 0)), (C2_A, "dup", 64, ("ka", 1)), (C2_A, "tok", 128, ("va", 0)),
         (C2_A, "feat", 256, ("u", 0)), (C2_A, "feat", 384, ("u", 1)),
         (C2_B, "feat", 0, ("u", 2)), (C2_B, "feat", 128, ("u", 3)),
         (C2_B, "feat", 256, ("qm", 0)), (C2_B, "feat", 384, ("qm", 1))]
        + [(C2_QA, "feat", 128 * i, ("qa", i)) for i in range(4)]
        + [(C2_QM, "feat", 128 * i, ("qm", 2 + i)) for i in range(2)]
        + [(C2_QM, "dup", 256, ("km", 0)), (C2_QM, "dup", 320, ("km", 1)), (C2_QM, "tok", 384, ("vm", 0))]
        + [(C2_GATE + i // 4, "feat", 128 * (i % 4), ("gate", i)) for i in range(24)])
CHUNK_ITEMS = [[t for t, p in enumerate(PROJ) if p[0] == c] for c in range(C2_SWA)]
ROUNDS = 8
U_ITEM = {j: t for t, p in enumerate(PROJ) for j in range(4) if p[3] == ("u", j)}


def round_items(r):
    return CHUNK_ITEMS[C2_QA + r] if r < ROUNDS else []



def build(nc, A, out):
    with ExitStack() as ctx:
        def sb(name, *shape, dt=F32):
            return ctx.enter_context(nc.sbuf_tensor(name, list(shape), dt))

        def sem(name):
            return ctx.enter_context(nc.semaphore(name))

        s_small_in = sem("small_in")
        s_x_in = sem("x_in")
        s_w_in0 = sem("w_in0")
        s_w_in1 = sem("w_in1")
        s_w_in2 = sem("w_in2")
        s_w2_in0 = sem("w2_in0")
        s_w2_in1 = sem("w2_in1")
        s_w2_in2 = sem("w2_in2")
        s_mixer_in = sem("mixer_in")
        s_ssm_in = sem("ssm_in")
        s_ones_ready = sem("ones_ready")
        s_silu_c = sem("silu_c")
        s_ada_used = sem("ada_used")
        s_ada_row = sem("ada_row")
        s_ada_cols = sem("ada_cols")
        s_mod_ready = sem("mod_ready")
        s_norm_sq = sem("norm_sq")
        s_norm_sum = sem("norm_sum")
        s_norm_std = sem("norm_std")
        s_norm_scaled = sem("norm_scaled")
        s_h_ready = sem("h_ready")
        s_x_updated = sem("x_updated")
        s_z_ready = sem("z_ready")
        s_sig_ready = sem("sig_ready")
        s_pad_zero = sem("pad_zero")
        s_a_ready = sem("a_ready")
        s_v_act = sem("v_act")
        s_v_var = sem("v_var")
        s_v_std = sem("v_std")
        s_v_ln = sem("v_ln")
        s_u_act = sem("u_act")
        s_sgu_ready = sem("sgu_ready")
        s_bo_ready = sem("bo_ready")
        s_conv_ready = sem("conv_ready")
        s_lna_sum = sem("lna_sum")
        s_lna_mean = sem("lna_mean")
        s_lna_centered = sem("lna_centered")
        s_lna_sq = sem("lna_sq")
        s_lna_std = sem("lna_std")
        s_lna_scaled = sem("lna_scaled")
        s_cat_ready = sem("cat_ready")
        s_mix_ready = sem("mix_ready")
        s_ffn_up = sem("ffn_up")
        s_ffn_silu = sem("ffn_silu")
        s_ffn_free = sem("ffn_free")
        s_ffn_down = sem("ffn_down")
        s_lat_ready = sem("lat_ready")
        s_lat_sb = sem("lat_sb")
        s_rot_ready = sem("rot_ready")
        s_kpe_ready = sem("kpe_ready")
        s_kn_ready = sem("kn_ready")
        s_kn_sb = sem("kn_sb")
        s_v_ready = sem("v_ready")
        s_v_sb = sem("v_sb")
        s_q_ready = sem("q_ready")
        s_q_sb = sem("q_sb")
        s_qr_ready = sem("qr_ready")
        s_s_ready = sem("s_ready")
        s_m_ready = sem("m_ready")
        s_exp_ready = sem("exp_ready")
        s_p_ready = sem("p_ready")
        s_pt_ready = sem("pt_ready")
        s_pt_sb = sem("pt_sb")
        s_pv_ready = sem("pv_ready")
        s_o_sb = sem("o_sb")
        s_wo_ready = sem("wo_ready")
        s_logits_ready = sem("logits_ready")
        s_htok_t = sem("htok_t")
        s_htok_sb = sem("htok_sb")
        s_gap_ready = sem("gap_ready")
        s_gap_exp = sem("gap_exp")
        s_masks_ready = sem("masks_ready")
        s_rank_ready = sem("rank_ready")
        s_items_ready = sem("items_ready")
        s_htok_hi = sem("htok_hi")
        s_select_ready = sem("select_ready")
        s_gather_ready = sem("gather_ready")
        s_xg_hi = sem("xg_hi")
        s_xg_ready = sem("xg_ready")
        s_put_turned = sem("put_turned")
        s_put_sb = sem("put_sb")
        s_split_hi = sem("split_hi")
        s_split_lo = sem("split_lo")
        s_quarter_used = sem("quarter_used")
        s_up_silu = sem("up_silu")
        s_eh_ready = sem("eh_ready")
        s_ht_ready = sem("ht_ready")
        s_he_hi = sem("he_hi")
        s_he_ready = sem("he_ready")
        s_ye_sb = sem("ye_sb")
        s_y_ready = sem("y_ready")
        s_y_added = sem("y_added")
        s_y_zero = sem("y_zero")
        s_ssm_theta = sem("ssm_theta")
        s_ssm_theta2 = sem("ssm_theta2")
        s_ssm_sin = sem("ssm_sin")
        s_ssm_f = sem("ssm_f")
        s_ssm_expanded = sem("ssm_expanded")
        s_e_ready = sem("e_ready")
        s_bb_t = sem("bb_t")
        s_bb_sb = sem("bb_sb")
        s_proj_ready = sem("proj_ready")
        s_proj_sb = sem("proj_sb")
        s_xs_ready = sem("xs_ready")
        s_xs_used = sem("xs_used")
        s_hs_ready = sem("hs_ready")
        s_y_psum = sem("y_psum")
        s_y_sb = sem("y_sb")
        s_as_ready = sem("as_ready")
        s_am_ready = sem("am_ready")
        s_ae_ready = sem("ae_ready")
        s_ap_ready = sem("ap_ready")
        s_apt_ready = sem("apt_ready")
        s_apt_sb = sem("apt_sb")
        s_ao_ready = sem("ao_ready")
        s_ao_sb = sem("ao_sb")
        s_br_ready = sem("br_ready")
        s_glu_sig = sem("glu_sig")
        s_br_free = sem("br_free")
        s_wout_ready = sem("wout_ready")
        s_ff1_ready = sem("ff1_ready")
        s_ff1_relu = sem("ff1_relu")
        s_ff1_free = sem("ff1_free")
        s_ff2_used = sem("ff2_used")
        s_out_stored = sem("out_stored")
        s_diag_ready = sem("diag_ready")
        w_in = [s_w_in0, s_w_in1, s_w_in2]
        w2_in = [s_w2_in0, s_w2_in1, s_w2_in2]

        psum = ctx.enter_context(nc.psum_tensor("psum", [P, 8, 512], F32))

        def bank(b):
            return psum[:, b, :]

        def bank2(b):
            return psum[:, b, :].rearrange("p (s t) -> p s t", s=2)

        ring = sb("ring", P, RING, SLOT)
        X = sb("X", P, 2, KT, T)
        H = sb("H", P, 2, KT, T)
        const = sb("const", P, N_CONST)
        param = sb("param", P, N_PARAM)
        ones = sb("ones", P, P)
        mod = sb("mod", P, DEPTH, 48, 2)
        gain = sb("gain", P, 4, KT, 2)
        rstd = sb("rstd", P, 2, 512)
        silu_c = sb("silu_c", P, KT, 2)
        small = sb("small", P, 400)

        def ctx_half(t):
            return t[:, 1].rearrange("p k t -> p (k t)").rearrange("p (i c) -> p i c", i=SSM_TILES)

        def cn(name):
            a, b = CONST_COLS[name]
            return const[:, a:b]

        def pr(name):
            a, b = PARAM_COLS[name]
            return param[:, a:b]

        ident = cn("ident")

        def placed(memory, at, shape):
            n = int(np.prod(shape))
            v = memory[:, at:at + n]
            if len(shape) == 2:
                v = v.rearrange("p (a b) -> p a b", a=shape[0])
            if len(shape) == 3:
                v = v.rearrange("p (a b c) -> p a b c", a=shape[0], b=shape[1])
            return v

        item_list = sb("item_list", P, 4, dt=I32)
        with nc.sbuf_tensor("region", [P, REGION], F32) as region:
            pass
        region_r = sb("region_r", P, REGION, dt=F32R)

        def reg(at, *shape):
            return placed(region, at, shape)

        def reg_r(at, *shape):
            return placed(region_r, at, shape)

        sq = reg(0, KT, 512)
        apad = reg(4096, 4, 2, T + 2 * PAD)
        cat = reg(6400, KT, 512)
        vln = reg(10496, 4, 512)
        sig = reg(12544, 4, 512)
        mixer_small = reg(14592, 2560)
        ln_v_g, ln_v_b = reg(14592, 512), reg(15104, 512)
        w_sT = reg(15616, B_HEADS, P)
        b_s = reg(16640, 4, P)
        ada_rows = reg(17152, RING, 512)
        ffn_h = reg(0, FT, 512)
        ffn_s = reg(11264, 3, 512)
        sq_ffn = reg(13312, KT, 512)
        probs, probsT = reg(0, 3, 512), reg(1536, 3, 4, P)
        q_lat = reg(4096, 1, 3, T)
        kv_lat = reg(4864, 2, 2, T)
        k_pe = reg(5888, 2, T)
        q_n, q_r = reg(6400, KT, T), reg(8448, KT, T)
        k_n = reg(10496, KT, 2, T)
        v_tok = reg(14592, 4, D)
        o_T = reg(18688, KT, T)
        rot_t = reg(20736, KT, T)
        h_hi, h_lo = reg_r(0, 2, D), reg_r(2048, 2, D)
        x_hi, x_lo = reg_r(4096, KT, P), reg_r(5120, KT, P)
        he_hi, he_lo = reg_r(6144, ET, P), reg_r(9728, ET, P)
        w_hi, w_lo = reg_r(13312, SPLIT, QUARTER), reg_r(17408, SPLIT, QUARTER)
        sq_moe = reg(6144, KT, T)
        e_silu, e_h = reg(21504, 2, 256), reg(22016, 2, 256)
        ye = rstd.rearrange("p a b -> p (a b)")
        putT = reg(22528, T)
        put = reg(22784, 2, P)
        pick = reg_r(23040, 2, P)
        y_T = reg(23296, KT, T)
        rot_re, rot_im = ctx_half(X), ctx_half(H)
        tmp_a, tmp_b = reg(22784, 1024), reg(23808, 1024)
        b_wide = reg(11520, 2, SSM_TILES, P)
        c_wide = reg(17408, 2, SSM_TILES, P)
        b_part = reg(0, 4, SSM_TILES, 16)
        ssm_raw = reg(21504, 4, SSM_TILES, 16)
        bb_T = reg(21504, 2, SSM_TILES, P)
        gates = reg(0, 24, T)
        qa, ka, va = reg(6144, 4, T), reg(7168, 2, T), reg(7680, 2, P)
        qm, km, vm = reg(7936, 4, T), reg(8960, 2, T), reg(9472, 2, P)
        u_T = reg(9728, 4, T)
        p2, pT2 = reg(10752, 2, 384), reg(11520, 2, 384)
        ssm_w = reg(12288, 2, 2, T)
        ssm_t = reg(13312, 2, 2, T)
        ssm_h = reg(14336, 2, 4, T)
        diag_d = reg(16384, 4, P)
        sq2 = reg(12288, KT, T)
        mixed = reg(17408, KT, T)
        glu_s, glu_z = reg(19456, 2, T), reg(19968, 4, T)
        mix_t = reg(10752, 2, T)
        ff_h, ff_relu = reg(0, 32, T), reg(8192, 6, T)

        def sm(at, *shape):
            v = small[:, at:at + int(np.prod(shape))]
            if len(shape) == 2:
                v = v.rearrange("p (a b) -> p a b", a=shape[0])
            return v

        v_stats, v_mv, v_rs = sm(0, 4, 6), sm(24, 4, 2), sm(32, 4)
        row_max, neg_max, row_sum = sm(36, 4), sm(40, 4), sm(44, 4)
        logits, work8, eq8 = sm(48, 2, 8), sm(64, 2, 8), sm(80, 2, 8)
        first8, second8 = sm(96, 2, 8), sm(112, 2, 8)
        mask8, gate8, rank8 = sm(128, 2, 8), sm(144, 2, 8), sm(160, 2, 8)
        top1, top2, where1, gap, g1, g2 = (sm(176 + 2 * i, 2) for i in range(6))
        over8, place8 = sm(188, 8), sm(304, 8)
        chosen_f = sm(312, 4)
        item_rank, item_mask, item_gate = (sm(312 + 4 + 24 * i, 2, N_ITEMS + 1) for i in range(3))
        a_max, a_neg, a_sum, a_sink = sm(198, 2, 2), sm(202, 2, 2), sm(206, 2, 2), sm(210, 2, 2)
        sink8 = sm(214, 8)
        mag, f_re, f_im = sm(224, 16), sm(240, 16), sm(256, 16)
        sin1, cos1 = sm(272, 16), sm(288, 16)
        scr = sb("scr", P, 10, 16)

        block = ctx.enter_context(nc.Block())

        def slot(n, k=KT, width=None):
            v = ring[:, n % RING, :]
            width = width or SLOT // k
            return v[:, 0:k * width].rearrange("p (k n) -> p k n", k=k)

        def cols(w, c, n, rows=None):
            w = w if rows is None else w[rows[0]:rows[1], :]
            return w[:, bass.ds(c, n)].rearrange("(k p) n -> p k n", p=P)

        @block.sync
        def _(sp):
            sp.dma_start(const[:, :], A["const"]).then_inc(s_small_in, 16)
            sp.dma_start(param[:, :], A["param"]).then_inc(s_small_in, 16)
            sp.dma_start(X[:, :, :, :], A["x"].rearrange("p (s k t) -> p s k t", s=2, k=KT)).then_inc(s_x_in, 16)
            sp.dma_start(mixer_small, A["mixer"]).then_inc(s_mixer_in, 16)

            def put_in(n, dst, src):
                sp.dma_start(dst, src).then_inc(w_in[n % RING], 16)

            def ada(n, layer, c):
                put_in(n, slot(n), cols(A["w_ada"][layer], c, 512))

            for n in range(RING):
                ada(n, 0, 512 * n)
            with sp.Fori(1, 12 // RING) as i:
                for q in range(RING):
                    sp.wait_ge(s_ada_used, RING * i + q - RING + 1)
                    ada(q, 0, 512 * (RING * i + q))
            for q, c in enumerate((0, 512, 1536, 1024)):
                if q < RING:
                    sp.wait_ge(s_ada_used, CH_Z + q - RING + 1)
                else:
                    sp.wait_ge(s_z_ready, 4 * (q - RING + 1))
                put_in(CH_Z + q, slot(CH_Z + q), cols(A["e_w_in"][0], c, 512))
            for q in range(RING):
                sp.wait_ge(s_z_ready, 4 * (q + 2))
                ada(CH_ADA1 + q, 1, 512 * q)
            with sp.Fori(1, 12 // RING) as i:
                for q in range(RING):
                    sp.wait_ge(s_ada_used, 12 + RING * i + q - RING + 1)
                    ada(CH_ADA1 + q, 1, 512 * (RING * i + q))
            for q in range(2):
                sp.wait_ge(s_ada_used, 24 - RING + q + 1)
                put_in(CH_OUT0 + q, slot(CH_OUT0 + q), cols(A["e_w_out"][0], 512 * q, 512))

            def up(n, c, w1, w3):
                put_in(n, slot(n)[:, :, 0:256], cols(w1, c, 256))
                put_in(n, slot(n)[:, :, 256:512], cols(w3, c, 256))

            for q in range(D_FF // 256):
                if q == 0:
                    sp.wait_ge(s_ada_used, 24)
                elif q < RING:
                    sp.wait_ge(s_mix_ready, 4 * q)
                else:
                    sp.wait_ge(s_ffn_up, 4 * (q - RING + 1))
                up(CH_UP + q, 256 * q, A["e_ffn_w1"][0], A["e_ffn_w3"][0])
            for q in range(6):
                r0 = 1024 * (q % 3)
                r1 = min(r0 + 1024, D_FF)
                n = CH_DOWN + q
                if q < RING:
                    sp.wait_ge(s_ffn_up, 4 * (D_FF // 256 - RING + q + 1))
                else:
                    sp.wait_ge(s_ffn_down, q - RING + 1)
                put_in(n, slot(n, (r1 - r0) // P, 512), cols(A["e_ffn_w2"][0], 512 * (q // 3), 512, (r0, r1)))
            sp.wait_ge(s_ffn_down, 4)
            put_in(CH_KV, slot(CH_KV, KT, 320), cols(A["o_w_in"][0], Q_RANK, KV_RANK + ROPE))
            sp.wait_ge(s_ffn_down, 5)
            put_in(CH_Q, slot(CH_Q, KT, Q_RANK), cols(A["o_w_in"][0], 0, Q_RANK))
            sp.wait_ge(s_ffn_down, 6)
            put_in(CH_UKV, slot(CH_UKV, 2, 2048), cols(A["o_w_ukv"][0], 0, 2048))
            for q in range(2):
                sp.wait_ge(s_lat_ready, 3 * (q + 1))
                put_in(CH_UQ + q, slot(CH_UQ + q, 3, 768), cols(A["o_w_uq"][0], 768 * q, 768))
            sp.wait_ge(s_v_ready, 8)
            put_in(CH_WO, slot(CH_WO), cols(A["o_w_o"][0], 0, 512))
            sp.wait_ge(s_q_ready, 4)
            put_in(CH_WO + 1, slot(CH_WO + 1), cols(A["o_w_o"][0], 512, 512))

            def expert(e, it, first=False):
                for j in range(PER_EXPERT):
                    if first and j < RING:
                        sp.wait_ge(*((s_q_ready, MLA_HEADS), (s_wo_ready, 4), (s_wo_ready, 8))[j])
                    else:
                        sp.wait_ge(s_split_lo, QUARTERS * it + 4 * (j - RING + 1))
                    if j < UPS:
                        up(j, 256 * j, A["o_exp_w1"][0, e], A["o_exp_w3"][0, e])
                    else:
                        d = j - UPS
                        put_in(j, slot(j, 4, D), A["o_exp_w2"][0, e, 512 * d:512 * d + 512, :].rearrange(
                            "(k p) n -> p k n", p=P))

            expert(0, 0, first=True)
            with sp.Fori(1, N_EXPERTS) as e:
                expert(e, e)
            sp.wait_ge(s_items_ready, 1)
            n_items = sp.value_load(item_list[0:1, 3:4], min_val=N_EXPERTS, max_val=N_ITEMS)
            for s in range(SPARE):
                with sp.If(n_items > N_EXPERTS + s):
                    e = sp.value_load(item_list[0:1, s:s + 1], min_val=0, max_val=N_EXPERTS - 1)
                    expert(e, N_EXPERTS + s)

            def put_in2(n, dst, src):
                sp.dma_start(dst, src).then_inc(w2_in[n % RING], 16)

            w_in_cols = {C2_A: 512, C2_B: 1024, C2_QA: 0, C2_QM: 1536}
            sp.wait_ge(s_x_updated, X_MIX1 + 1)
            for n in range(C2_SWA):
                if n >= RING:
                    sp.wait_ge(s_proj_ready, CHUNK_ITEMS[n - RING][-1] + 1)
                put_in2(n, slot(n), cols(A["w_in_2"][0], w_in_cols.get(n, 2048 + 512 * (n - C2_GATE)), 512))
            for n, w in ((C2_SWA, "w_o_swa_2"), (C2_MOBA, "w_o_moba_2"), (C2_GLU, "w_glu_2"), (C2_SSM, "w_o_ssm_2")):
                if n < C2_SWA + RING:
                    sp.wait_ge(s_proj_ready, CHUNK_ITEMS[n - RING][-1] + 1)
                else:
                    sp.wait_ge(s_br_ready, 8 * (n - RING - C2_SWA + 1))
                put_in2(n, slot(n, 4, D), cols(A[w][0], 0, D))
            for q in range(2):
                sp.wait_ge(s_br_ready, 8 * (q + 2))
                put_in2(C2_OUT + q, slot(C2_OUT + q), cols(A["w_out_2"][0], 512 * q, 512))
            for q in range(8):
                if q == 0:
                    sp.wait_ge(s_br_ready, 32)
                elif q < RING:
                    sp.wait_ge(s_wout_ready, 4 * q)
                else:
                    sp.wait_ge(s_ff1_ready, 4 * (q - RING + 1))
                put_in2(C2_FF1 + q, slot(C2_FF1 + q), cols(A["w_ff1_2"][0], 512 * q, 512))
            for q in range(8):
                if q < RING:
                    sp.wait_ge(s_ff1_ready, 4 * (8 - RING + q + 1))
                else:
                    sp.wait_ge(s_ff2_used, q - RING + 1)
                put_in2(C2_FF2 + q, slot(C2_FF2 + q, 4, D), cols(A["w_ff2_2"][0], 0, D, (512 * q, 512 * q + 512)))
            sp.wait_ge(s_h_ready, tiles_before(N_END2) + KT)
            sp.dma_start(out, H[:, 0, :, :].rearrange("p k t -> p (k t)")).then_inc(s_out_stored, 16)
            sp.wait_ge(s_out_stored, 16)

        @block.tensor
        def _(pe):
            def group(dst, pairs):
                for i, (lhsT, rhs) in enumerate(pairs):
                    mm = pe.matmul(dst, lhsT, rhs, start=(i == 0), stop=(i == len(pairs) - 1))
                return mm

            def norm(n, squares):
                kt, sets, _ = NORMS[n]
                w = sets * T
                if n:
                    pe.wait_ge(s_norm_std, n)
                for k in range(kt):
                    pe.wait_ge(s_norm_sq, tiles_before(n) + k + 1)
                    mm = pe.matmul(bank(7)[:, 0:w], ones[:, :], squares[:, k, 0:w], start=(k == 0), stop=(k == kt - 1))
                mm.then_inc(s_norm_sum, 1)

            def h_tiles(n):
                pe.wait_ge(s_h_ready, tiles_before(n) + NORMS[n][0])

            pe.wait_ge(s_small_in, 32)
            pe.wait_ge(s_ones_ready, 1)
            norm(N_MIX0, sq)

            def ada_three(layer, first, j, ready):
                def turn(q):
                    pe.wait_ge(s_ada_row, 12 * layer + j + q + 1)
                    for i in range(4):
                        mm = pe.matmul(psum[:, 2, bass.ds(8 * (j + q) + 2 * i, 2)], ada_rows[0:2, q, i * P:(i + 1) * P],
                                       ident[0:2, 0:2], start=True, stop=True)
                    mm.then_inc(s_ada_cols, 1)

                for q in range(RING):
                    ready(q)
                    group(psum[0:2, ADA_BANKS[q], :], [(silu_c[:, k, :], slot(first + q)[:, k, :]) for k in range(KT)]
                          ).then_inc(s_ada_used, 1)
                    if q:
                        turn(q - 1)
                turn(RING - 1)

            pe.wait_ge(s_silu_c, 1)
            with pe.Fori(0, 12 // RING) as i:
                ada_three(0, 0, RING * i, lambda q: pe.wait_ge(w_in[q], 16 * i + 16))

            h_tiles(N_MIX0)
            for c in range(2):
                n = CH_Z + c
                pe.wait_ge(w_in[n % RING], landed(n))
                if c == 0:
                    pe.wait_ge(s_mod_ready, 1)
                else:
                    pe.wait_ge(s_norm_std, 1)
                for i in range(4):
                    group(bank2(4 * c + i), [(slot(n)[:, k, i * P:(i + 1) * P], H[:, :, k, :]) for k in range(KT)]
                          ).then_inc(s_z_ready, 1)
            n = CH_Z + 2
            pe.wait_ge(w_in[n % RING], landed(n))
            for t in range(4):
                pe.wait_ge(s_sig_ready, t + 1)
                group(bank(4 + t), [(H[:, t // 2, k, (t % 2) * P:(t % 2 + 1) * P], slot(n)[:, k, :]) for k in range(KT)]
                      ).then_inc(s_z_ready, 1)
            n = CH_Z + 3
            pe.wait_ge(w_in[n % RING], landed(n))
            for i in range(4):
                pe.wait_ge(s_a_ready, i + 1)
                group(bank2(i), [(slot(n)[:, k, i * P:(i + 1) * P], H[:, :, k, :]) for k in range(KT)]
                      ).then_inc(s_z_ready, 1)
            pe.wait_ge(s_mixer_in, 16)
            pe.wait_ge(s_v_ln, 4)
            for j in range(4):
                for half in range(2):
                    h = 2 * j + half
                    for t in range(4):
                        mm = pe.matmul(psum[64 * half:64 * half + 64, 4 + j, t * P:(t + 1) * P],
                                       vln[:, t, h * 64:h * 64 + 64], w_sT[:, h, :], start=True, stop=True)
                mm.then_inc(s_sgu_ready, 1)
            pe.wait_ge(s_u_act, 4)
            with pe.Fori(0, 12 // RING) as i:
                ada_three(1, CH_ADA1, RING * i,
                          lambda q: pe.wait_ge(w_in[(CH_ADA1 + q) % RING], 16 * i + landed(CH_ADA1 + q)))
            for i in range(4):
                pe.wait_ge(s_conv_ready, i + 1)
                mm = pe.matmul(bank(0), ones[:, :], cat[:, i, :], start=(i == 0), stop=(i == 3))
            mm.then_inc(s_lna_sum, 1)
            for i in range(4):
                pe.wait_ge(s_lna_sq, i + 1)
                mm = pe.matmul(bank(3), ones[:, :], sq[:, i, :], start=(i == 0), stop=(i == 3))
            mm.then_inc(s_lna_sum, 1)
            pe.wait_ge(s_bo_ready, 4)
            pe.wait_ge(s_cat_ready, 4)
            pe.wait_ge(s_mod_ready, 2)
            for i in range(8):
                n = CH_OUT0 + i // 4
                if i % 4 == 0:
                    pe.wait_ge(w_in[n % RING], landed(n))
                c = (i % 4) * P
                group(bank(i), [(slot(n)[:, k, c:c + P], cat[:, k, :]) for k in range(KT)]).then_inc(s_mix_ready, 1)

            pe.wait_ge(s_x_updated, X_MIX0)
            norm(N_FFN0, sq_ffn)
            h_tiles(N_FFN0)

            def ffn_up(n, at, first):
                for i in range(2):
                    b = 2 * ((first + i) % 3)
                    pe.wait_ge(s_ffn_free, at + i + 1)
                    for w in range(2):
                        c = 256 * w + P * i
                        group(bank2(b + w), [(slot(n)[:, k, c:c + P], H[:, :, k, :]) for k in range(KT)]
                              ).then_inc(s_ffn_up, 1)

            with pe.Fori(0, 3) as i:
                for q in range(RING):
                    n = CH_UP + q
                    pe.wait_ge(w_in[n % RING], 32 * i + landed(n))
                    ffn_up(n, 6 * i + 2 * q, 2 * q)
            for q in range(9, 11):
                n = CH_UP + q
                pe.wait_ge(w_in[n % RING], landed(n))
                ffn_up(n, 2 * q, 2 * q)
            pe.wait_ge(s_ffn_free, FT + 3)
            for half in range(2):
                for g in range(3):
                    n = CH_DOWN + 3 * half + g
                    k0, k1 = 8 * g, min(8 * g + 8, FT)
                    pe.wait_ge(w_in[n % RING], landed(n))
                    w = slot(n, k1 - k0, 512)
                    if half and g == 0:
                        pe.wait_ge(s_norm_std, N_FFN0 + 1)
                    for i in range(4):
                        for k in range(k0, k1):
                            mm = pe.matmul(bank(4 * half + i), w[:, k - k0, i * P:(i + 1) * P], ffn_h[:, k, :],
                                           start=(k == 0), stop=(k == FT - 1))
                    mm.then_inc(s_ffn_down, 1)

            pe.wait_ge(s_x_updated, X_FFN0)
            norm(N_MIX1, sq_ffn)
            h_tiles(N_MIX1)
            n = CH_KV
            pe.wait_ge(w_in[n % RING], landed(n))
            for i in range(2):
                group(bank2(i), [(slot(n, KT, 320)[:, k, i * P:(i + 1) * P], H[:, :, k, :]) for k in range(KT)]
                      ).then_inc(s_lat_ready, 1)
            group(bank2(2)[0:64], [(slot(n, KT, 320)[:, k, 256:320], H[:, :, k, :]) for k in range(KT)]
                  ).then_inc(s_lat_ready, 1)
            n = CH_Q
            pe.wait_ge(w_in[n % RING], landed(n))
            for i in range(3):
                group(bank(3 + i)[:, 0:T], [(slot(n, KT, Q_RANK)[:, k, i * P:(i + 1) * P], H[:, 0, k, :]) for k in range(KT)]
                      ).then_inc(s_lat_ready, 1)
            norm(N_KV, sq)
            norm(N_Q, sq)
            pe.wait_ge(s_lat_sb, 6)
            pe.matmul(psum[0:64, 2, 0:T], cn("rot")[0:64, :], k_pe[0:64, 0, :], start=True, stop=True).then_inc(s_rot_ready, 1)
            n = CH_UKV
            pe.wait_ge(w_in[n % RING], landed(n))
            h_tiles(N_KV)
            pe.wait_ge(s_kpe_ready, 1)
            w = slot(n, 2, 2048)
            for h in range(MLA_HEADS):
                if h >= 4:
                    pe.wait_ge(s_kn_sb, h - 3)
                group(bank2(h % 4), [(w[:, k, 256 * h:256 * h + P], kv_lat[:, :, k, :]) for k in range(2)]
                      ).then_inc(s_kn_ready, 1)
            for t in range(4):
                for half in range(2):
                    i = 2 * t + half
                    if i >= 3:
                        pe.wait_ge(s_v_sb, i - 2)
                    wv = [w[:, k, 1024 * half:1024 * half + 1024].rearrange("p (h c) -> p h c", h=4)[:, :, P:2 * P]
                          for k in range(2)]
                    group(psum[:, 4 + i % 3, :].rearrange("p (h c) -> p h c", h=4),
                          [(kv_lat[:, t // 2, k, (t % 2) * P:(t % 2 + 1) * P], wv[k]) for k in range(2)]
                          ).then_inc(s_v_ready, 1)
            h_tiles(N_Q)
            for h in range(MLA_HEADS):
                n = CH_UQ + h // 4
                if h % 4 == 0:
                    pe.wait_ge(w_in[n % RING], landed(n))
                if h < 4:
                    pe.wait_ge(s_kn_sb, h + 5)
                else:
                    pe.wait_ge(s_q_sb, h - 3)
                w = slot(n, 3, 768)
                c = 192 * (h % 4)
                group(bank(h % 4)[:, 0:T], [(w[:, k, c:c + P], q_lat[:, 0, k, :]) for k in range(3)])
                group(bank(h % 4)[0:64, T:2 * T], [(w[:, k, c + P:c + P + ROPE], q_lat[:, 0, k, :]) for k in range(3)]
                      ).then_inc(s_q_ready, 1)
            for i in range(4):
                pe.wait_ge(s_q_sb, 2 * i + 2)
                if i < 3:
                    pe.wait_ge(s_v_sb, 8)
                else:
                    pe.wait_ge(s_qr_ready, 1)
                pe.matmul(psum[0:64, 4 + i % 3, :].rearrange("p (h t) -> p h t", h=2), cn("rot")[0:64, :],
                          q_r[0:64, 2 * i:2 * i + 2, :], start=True, stop=True).then_inc(s_rot_ready, 1)
            pe.wait_ge(s_q_sb, 8)
            pe.wait_ge(s_qr_ready, 4)
            UNITS = 2 * MLA_HEADS
            for u in range(UNITS + 3):
                if u < UNITS:
                    h, q0 = u // 2, (u % 2) * P
                    if u >= 3:
                        pe.wait_ge(s_exp_ready, u - 2)
                    pe.matmul(bank2(u % 3), q_n[:, h, q0:q0 + P], k_n[:, h, :, :], start=True, stop=False)
                    pe.matmul(bank2(u % 3), q_r[0:64, h, q0:q0 + P], k_pe[0:64, :, :], start=False, stop=True
                              ).then_inc(s_s_ready, 1)
                if 2 <= u < UNITS + 2:
                    v = u - 2
                    pe.wait_ge(s_p_ready, v + 1)
                    if v >= 2:
                        pe.wait_ge(s_pt_sb, v - 1)
                    for i in range(4):
                        mm = pe.transpose(psum[:, 3 + v % 2, i * P:(i + 1) * P], probs[:, v % 3, i * P:(i + 1) * P], ident)
                    mm.then_inc(s_pt_ready, 1)
                if u >= 3:
                    v = u - 3
                    h, q0 = v // 2, (v % 2) * P
                    pe.wait_ge(s_pt_sb, v + 1)
                    if h >= 2:
                        pe.wait_ge(s_o_sb, h - 1)
                    group(psum[:, 5 + h % 2, q0:q0 + P], [(v_tok[:, i, h * P:(h + 1) * P], probsT[:, v % 3, i, :]) for i in range(4)]
                          ).then_inc(s_pv_ready, 1)
            pe.wait_ge(s_o_sb, MLA_HEADS)
            for i in range(8):
                n = CH_WO + i // 4
                if i % 4 == 0:
                    pe.wait_ge(w_in[n % RING], landed(n))
                c = (i % 4) * P
                mm = group(bank(i)[:, 0:T], [(slot(n)[:, k, c:c + P], o_T[:, k, :]) for k in range(KT)])
                mm.then_inc(s_wo_ready, 1)
            pe.wait_ge(s_x_updated, X_MIX1)
            pe.sem_inc(s_quarter_used, SPLIT)
            norm(N_MOE, sq_moe)
            h_tiles(N_MOE)
            for t in range(2):
                mm = group(bank(0)[:, 8 * t:8 * t + 8], [(H[:, 0, k, t * P:(t + 1) * P],
                           pr("router").rearrange("p (k e) -> p k e", k=KT)[:, k, :]) for k in range(KT)])
            mm.then_inc(s_logits_ready, 1)
            for i in range(4):
                for j in range(4):
                    t, k = divmod(4 * i + j, KT)
                    mm = pe.transpose(psum[:, 1 + i, j * P:(j + 1) * P], H[:, 0, k, t * P:(t + 1) * P], ident)
                mm.then_inc(s_htok_t, 1)
            pe.wait_ge(s_masks_ready, 1)
            group(bank(5)[:, 0:8], [(cn("tri"), mask8[:, 0, :])])
            group(bank(5)[:, 8:16], [(cn("tri"), mask8[:, 1, :]), (ones[:, :], mask8[:, 0, :])])
            group(bank(5)[:, 16:24], [(ones[:, :], mask8[:, 0, :]), (ones[:, :], mask8[:, 1, :])]).then_inc(s_rank_ready, 1)

            def product(out, parts, start, stop):
                for n, (a_hi, a_lo, b_hi, b_lo) in enumerate(parts):
                    first, last = start and n == 0, stop and n == len(parts) - 1
                    pe.matmul(out, a_hi, b_hi, start=first, stop=False)
                    pe.matmul(out, a_hi, b_lo, start=False, stop=False)
                    mm = pe.matmul(out, a_lo, b_hi, start=False, stop=last)
                return mm

            def gather(it):
                pe.wait_ge(s_select_ready, it + 1)
                for b in range(2):
                    for j in range(4):
                        k = 4 * b + j
                        mm = group(psum[:, b, j * P:(j + 1) * P],
                                   [(h[:, t, k * P:(k + 1) * P], pick[:, t, :]) for t in range(2) for h in (h_hi, h_lo)])
                    mm.then_inc(s_gather_ready, 1)

            def turn_put():
                for t in range(2):
                    mm = pe.transpose(psum[:, 6, t * P:(t + 1) * P], put[:, t, :], ident)
                mm.then_inc(s_put_turned, 1)

            def expert(it):
                def turn(j):
                    pe.wait_ge(s_eh_ready, UPS * it + j + 3)
                    pe.wait_ge(s_he_ready, UPS * it + j + 1)
                    if j < 2:
                        pe.wait_ge(s_y_added, 4 * it + 3 + j)
                    for i in range(2):
                        mm = pe.transpose(psum[:, 4 + j % 2, i * P:(i + 1) * P], e_h[:, j % 2, i * P:(i + 1) * P], ident)
                    mm.then_inc(s_ht_ready, 1)

                pe.wait_ge(s_xg_ready, 2 * it + 2)
                for q in range(QUARTERS):
                    b = q % SPLIT
                    pe.wait_ge(s_split_lo, QUARTERS * it + q + 1)
                    if q < UP_QUARTERS:
                        j = q // 4
                        if q % 4 == 0:
                            pe.wait_ge(s_eh_ready, UPS * it + j + 1)
                        w = [v[:, b, :].rearrange("p (k n) -> p k n", k=2) for v in (w_hi, w_lo)]
                        k0 = 2 * (q % 4)
                        mm = product(bank(j % 2), [(x_hi[:, k0 + k, :], x_lo[:, k0 + k, :], w[0][:, k, :], w[1][:, k, :])
                                                   for k in range(2)], q % 4 == 0, q % 4 == 3)
                    else:
                        i = q - UP_QUARTERS
                        if i == 0:
                            pe.wait_ge(s_put_sb, it + 1)
                        if i % 2 == 0:
                            pe.wait_ge(s_he_ready, UPS * it + i // 2 + 3)
                        for half in range(2):
                            c = slice(512 * half, 512 * half + 512)
                            mm = product(bank(6 + half), [(he_hi[:, i, :], he_lo[:, i, :], w_hi[:, b, c], w_lo[:, b, c])],
                                         i == 0, i == ET - 1)
                    mm.then_inc(s_quarter_used, 1)
                    if q % 4 == 3 and 7 <= q < UP_QUARTERS + 4:
                        turn(q // 4 - 1)
                gather(it + 1)
                pe.wait_ge(s_ye_sb, 2 * it + 2)
                pe.wait_ge(s_y_added, 4 * it + 4)
                for b in range(4):
                    for j in range(2):
                        i = 2 * b + j
                        mm = pe.matmul(psum[:, 2 + b, j * T:(j + 1) * T], ye[:, i * P:(i + 1) * P], putT, start=True, stop=True)
                    mm.then_inc(s_y_ready, 1)
                turn_put()

            pe.wait_ge(s_items_ready, 1)
            pe.wait_ge(s_htok_sb, 4)
            gather(0)
            turn_put()
            pe.wait_ge(s_y_zero, 1)
            for b in range(4):
                pe.matmul(bank(2 + b), ones[:, :], y_T[:, 0:2, :].rearrange("p k t -> p (k t)"), start=True, stop=True
                          ).then_inc(s_y_ready, 1)
            n_items = pe.value_load(item_list[0:1, 3:4], min_val=N_EXPERTS, max_val=N_ITEMS)
            with pe.Fori(0, n_items) as it:
                expert(it)

            pe.wait_ge(s_x_updated, X_MOE)
            norm(N_END1, sq_moe)
            norm(N_MIX2, sq_moe)
            h_tiles(N_MIX2)

            def project(t):
                n, kind, c, _ = PROJ[t]
                if t in (ci[0] for ci in CHUNK_ITEMS):
                    pe.wait_ge(w2_in[n % RING], 16 * (n // RING + 1))
                if t == 1:
                    pe.wait_ge(s_norm_std, N_MIX2 + 1)
                if t >= 2:
                    pe.wait_ge(s_proj_sb, t - 1)
                w, b = slot(n), bank(6 + t % 2)
                if kind == "feat":
                    mm = group(b[:, 0:T], [(w[:, k, c:c + P], H[:, 0, k, :]) for k in range(KT)])
                elif kind == "dup":
                    for half in range(2):
                        mm = group(b[64 * half:64 * half + 64, 0:T], [(w[:, k, c:c + HEAD], H[:, 0, k, :]) for k in range(KT)])
                else:
                    for i in range(2):
                        mm = group(b[:, i * P:(i + 1) * P], [(H[:, 0, k, i * P:(i + 1) * P], w[:, k, c:c + P]) for k in range(KT)])
                mm.then_inc(s_proj_ready, 1)

            def state_input(r):
                j = r // 2
                pe.wait_ge(s_proj_sb, U_ITEM[j] + 1)
                if r:
                    pe.wait_ge(s_xs_used, r)
                for v in range(2):
                    for i in range(2):
                        mm = pe.matmul(psum[:, 4 + v, i * T:(i + 1) * T], bb_T[:, v, 2 * r + i, :], u_T[:, j, :],
                                       start=True, stop=True)
                mm.then_inc(s_xs_ready, 1)

            def state_output(j):
                pe.wait_ge(s_hs_ready, 4 * (j + 1))
                pe.wait_ge(s_diag_ready, 1)
                if j:
                    pe.wait_ge(s_y_sb, j)
                pe.wait_ge(s_ao_sb, 2 * j + 1)
                pairs = [(c_wide[:, v, 4 * j + i, :], ssm_h[:, v, i, :]) for i in range(4) for v in range(2)]
                group(bank(3)[:, T:2 * T], pairs + [(diag_d[:, j, :], u_T[:, j, :])]).then_inc(s_y_psum, 1)

            def head_parts(a):
                q, k, v = (qa, ka, va) if a < 8 else (qm, km, vm)
                lo = 64 * (a % 2)
                return q[:, (a % 8) // 2, :], k, v, slice(lo, lo + 64), (a % 8) // 4

            def scores(a):
                q, k, _, rows, g = head_parts(a)
                if a >= 2:
                    pe.wait_ge(s_am_ready, a - 1)
                pe.matmul(bank(a % 2)[:, 0:P], q[rows, 0:P], k[rows, g, 0:P], start=True, stop=True)
                pe.matmul(bank(a % 2)[:, P:P + T], q[rows, P:T], k[rows, g, :], start=True, stop=True).then_inc(s_as_ready, 1)

            def turn2(a):
                pe.wait_ge(s_ap_ready, a + 1)
                if a:
                    pe.wait_ge(s_apt_sb, a)
                for i in range(3):
                    mm = pe.transpose(psum[:, 2, i * P:(i + 1) * P], p2[:, a % 2, i * P:(i + 1) * P], ident)
                mm.then_inc(s_apt_ready, 1)

            def values(a):
                _, _, v, rows, g = head_parts(a)
                pe.wait_ge(s_apt_sb, a + 1)
                if a >= 2 and a % 2 == 0:
                    pe.wait_ge(s_ao_sb, a // 2)
                    pe.wait_ge(s_y_sb, (a // 2 + 1) // 2)
                w = [v[:, i, g * HEAD:(g + 1) * HEAD] for i in range(2)]
                pt = [pT2[:, a % 2, i * P:(i + 1) * P] for i in range(3)]
                group(psum[rows, 3, 0:P], [(w[0], pt[0])])
                group(psum[rows, 3, P:T], [(w[0], pt[1]), (w[1], pt[2])]).then_inc(s_ao_ready, 1)

            for t in CHUNK_ITEMS[C2_A] + CHUNK_ITEMS[C2_B]:
                project(t)
            pe.wait_ge(s_ssm_expanded, 1)
            for i in range(8):
                if i >= 4:
                    pe.wait_ge(s_bb_sb, i - 3)
                for j in range(4):
                    v, k = divmod(4 * i + j, SSM_TILES)
                    mm = pe.transpose(psum[:, i % 4, j * P:(j + 1) * P], b_wide[:, v, k, :], ident)
                mm.then_inc(s_bb_t, 1)
            pe.wait_ge(s_bb_sb, 8)
            for r in range(ROUNDS + 1):
                items = round_items(r)
                if r < ROUNDS:
                    state_input(r)
                if items:
                    project(items[0])
                if r >= 2 and r % 2 == 0:
                    state_output(r // 2 - 1)
                if r:
                    pe.wait_ge(s_proj_sb, CHUNK_ITEMS[C2_QA if r <= 4 else C2_QM][-1] + 1)
                    scores(2 * r - 2)
                    scores(2 * r - 1)
                for t in items[1:3]:
                    project(t)
                if r:
                    turn2(2 * r - 2)
                for t in items[3:]:
                    project(t)
                if r:
                    turn2(2 * r - 1)
                    values(2 * r - 2)
                    values(2 * r - 1)

            def branch(n, first, src, order):
                pe.wait_ge(w2_in[n % RING], 16 * (n // RING + 1))
                w = slot(n, 4, D)
                for i, tile in enumerate(order):
                    g = first + i
                    if g >= 8:
                        pe.wait_ge(s_br_free, g - 7)
                    group(bank(g % 8)[:, 0:T], [(w[:, k, tile * P:(tile + 1) * P], src[:, k, :]) for k in range(4)]
                          ).then_inc(s_br_ready, 1)

            pe.wait_ge(s_proj_sb, len(PROJ))
            pe.wait_ge(s_ao_sb, 8)
            pe.wait_ge(s_y_sb, 4)
            pe.wait_ge(s_xs_used, ROUNDS)
            branch(C2_SWA, 0, qa, range(8))
            branch(C2_MOBA, 8, qm, range(8))
            branch(C2_GLU, 16, u_T, (4, 0, 5, 1, 6, 2, 7, 3))
            pe.wait_ge(s_br_free, 24)
            branch(C2_SSM, 24, glu_z, range(8))
            pe.wait_ge(s_br_free, 32)
            for i in range(8):
                n = C2_OUT + i // 4
                if i % 4 == 0:
                    pe.wait_ge(w2_in[n % RING], 16 * (n // RING + 1))
                c = (i % 4) * P
                group(bank(i)[:, 0:T], [(slot(n)[:, k, c:c + P], mixed[:, k, :]) for k in range(KT)]).then_inc(s_wout_ready, 1)

            pe.wait_ge(s_x_updated, X_MIX2)
            norm(N_FFN2, sq2)
            h_tiles(N_FFN2)

            def ff1(n, at):
                for i in range(4):
                    pe.wait_ge(s_ff1_free, at + i + 1)
                    group(bank((4 * (n - C2_FF1) + i) % 6)[:, 0:T],
                          [(slot(n)[:, k, i * P:(i + 1) * P], H[:, 0, k, :]) for k in range(KT)]).then_inc(s_ff1_ready, 1)

            with pe.Fori(0, 2) as i:
                for q in range(RING):
                    n = C2_FF1 + q
                    pe.wait_ge(w2_in[n % RING], 16 * i + 16 * (n // RING + 1))
                    ff1(n, 12 * i + 4 * q)
            for q in range(6, 8):
                n = C2_FF1 + q
                pe.wait_ge(w2_in[n % RING], 16 * (n // RING + 1))
                ff1(n, 4 * q)
            pe.wait_ge(s_ff1_free, 32 + 6)
            pe.wait_ge(s_norm_std, N_FFN2 + 1)

            def ff2(n, d, start, stop):
                for i in range(8):
                    for k in range(4):
                        mm = pe.matmul(bank(i)[:, 0:T], slot(n, 4, D)[:, k, i * P:(i + 1) * P],
                                       ff_h[:, bass.ds(4 * d + k, 1), :].rearrange("p a t -> p (a t)"),
                                       start=(start and k == 0), stop=(stop and k == 3))
                mm.then_inc(s_ff2_used, 1)

            pe.wait_ge(w2_in[C2_FF2 % RING], 16 * (C2_FF2 // RING + 1))
            ff2(C2_FF2, 0, True, False)
            with pe.Fori(0, 2) as i:
                for q in range(RING):
                    n = C2_FF2 + 1 + q
                    pe.wait_ge(w2_in[n % RING], 16 * i + 16 * (n // RING + 1))
                    ff2(n, RING * i + 1 + q, False, False)
            n = C2_FF2 + 7
            pe.wait_ge(w2_in[n % RING], 16 * (n // RING + 1))
            ff2(n, 7, False, True)
            pe.wait_ge(s_x_updated, X_FFN2)
            norm(N_END2, sq2)

        def norm_place(n):
            return {N_MIX0: (0, 0), N_FFN0: (0, 24), N_MIX1: (1, 0), N_MOE: (1, 24)}[n]

        @block.scalar
        def _(act):
            def norm(n, src, squares, ready, dim):
                kt, sets, _ = NORMS[n]
                w = sets * T
                for k in range(kt):
                    ready(k)
                    act.activation(squares[:, k, 0:w].rearrange("p (s t) -> p s t", s=sets), src[:, 0:sets, k, :], ACT.Square
                                   ).then_inc(s_norm_sq, 1)
                act.wait_ge(s_norm_sum, n + 1)
                act.activation(rstd[:, n % 2, 0:w], bank(7)[:, 0:w], ACT.Sqrt, bias=EPS, scale=1.0 / dim).then_inc(s_norm_std, 1)

            def shift(n):
                kt, sets, _ = NORMS[n]
                layer, at = norm_place(n)
                for k in range(kt):
                    act.wait_ge(s_norm_scaled, modulated_before(n) + k + 1)
                    for s in range(sets):
                        a = act.activation(H[:, s, k, :], H[:, s, k, :], ACT.Identity, bias=mod[:, layer, at + k, s:s + 1])
                    a.then_inc(s_h_ready, 1)

            def updated(base):
                return lambda k: act.wait_ge(s_x_updated, base + k + 1)

            def turned_over(k):
                if k == 0:
                    act.drain()

            act.wait_ge(s_small_in, 32)
            act.activation(silu_c[:, :, :].rearrange("p k s -> p (k s)"), pr("c"), ACT.Silu).then_inc(s_silu_c, 1)
            act.activation(scr[:, 0, :], pr("log_step"), ACT.Exp).then_inc(s_ssm_theta, 1)
            act.wait_ge(s_ssm_theta2, 1)
            act.activation(mag, scr[:, 1, :], ACT.Exp).then_inc(s_ssm_sin, 1)
            act.wait_ge(s_ssm_theta2, 2)
            act.activation(sin1, scr[:, 2, :], ACT.Sin)
            act.activation(scr[:, 3, :], scr[:, 2, :], ACT.Sin, scale=0.5).then_inc(s_ssm_sin, 1)

            norm(N_MIX0, X, sq, lambda k: act.wait_ge(s_x_in, 16), D)

            def ada_three(at):
                for q in range(RING):
                    act.wait_ge(s_ada_used, at + q + 1)
                    act.activation(ada_rows[0:2, q, :], psum[0:2, ADA_BANKS[q], :], ACT.Copy).then_inc(s_ada_row, 1)

            with act.Fori(0, 12 // RING) as i:
                ada_three(RING * i)
            shift(N_MIX0)
            for i in range(4):
                act.wait_ge(s_z_ready, 5 + i)
                act.activation(sig[:, i, :], bank(4 + i), ACT.Sigmoid).then_inc(s_sig_ready, 1)
            for i in range(4):
                act.wait_ge(s_z_ready, 9 + i)
                act.activation(vln[:, i, :], bank(4 + i), ACT.Gelu_apprx_tanh).then_inc(s_v_act, 1)
            act.wait_ge(s_v_var, 1)
            act.activation(v_rs, v_mv[:, :, 1], ACT.Sqrt, bias=EPS).then_inc(s_v_std, 1)
            for i in range(4):
                act.wait_ge(s_z_ready, 13 + i)
                act.activation(cat[:, 4 + i, :], bank(i), ACT.Gelu_apprx_tanh).then_inc(s_u_act, 1)
            with act.Fori(0, 12 // RING) as i:
                ada_three(12 + RING * i)
            act.wait_ge(s_lna_sum, 1)
            act.activation(rstd[:, 1, :], bank(0), ACT.Copy, scale=1.0 / 512).then_inc(s_lna_mean, 1)
            for i in range(4):
                act.wait_ge(s_lna_centered, i + 1)
                act.activation(sq[:, i, :], cat[:, i, :], ACT.Square).then_inc(s_lna_sq, 1)
            act.wait_ge(s_lna_sum, 2)
            act.activation(rstd[:, 0, :], bank(3), ACT.Sqrt, bias=EPS, scale=1.0 / 512).then_inc(s_lna_std, 1)
            for i in range(4):
                act.wait_ge(s_lna_scaled, i + 1)
                act.activation(cat[:, i, :], cat[:, i, :], ACT.Silu, bias=pr("ln_a_b")[:, i:i + 1],
                               scale=pr("ln_a_g")[:, i:i + 1]).then_inc(s_cat_ready, 1)

            norm(N_FFN0, X, sq_ffn, updated(0), D)
            shift(N_FFN0)

            def ffn_silu(at, i):
                act.wait_ge(s_ffn_up, 2 * at + 1)
                act.activation(ffn_s[:, i % 3, :], bank(2 * (i % 3)), ACT.Silu).then_inc(s_ffn_silu, 1)

            with act.Fori(0, 3) as g:
                for i in range(6):
                    ffn_silu(6 * g + i, i)
            for i in range(18, FT):
                ffn_silu(i, i)

            norm(N_MIX1, X, sq_ffn, updated(X_MIX0), D)
            shift(N_MIX1)
            for i in range(3):
                act.wait_ge(s_lat_ready, i + 1)
                dst = kv_lat[:, :, i, :] if i < 2 else k_pe[0:64, :, :]
                act.activation(dst, bank2(i) if i < 2 else bank2(2)[0:64], ACT.Copy).then_inc(s_lat_sb, 1)
            for i in range(3):
                act.wait_ge(s_lat_ready, i + 4)
                act.activation(q_lat[:, 0, i, :], bank(3 + i)[:, 0:T], ACT.Copy).then_inc(s_lat_sb, 1)
            norm(N_KV, kv_lat, sq, turned_over, KV_RANK)
            norm(N_Q, q_lat, sq, turned_over, Q_RANK)
            for h in range(MLA_HEADS):
                act.wait_ge(s_kn_ready, h + 1)
                act.activation(k_n[:, h, :, :], bank2(h % 4), ACT.Copy).then_inc(s_kn_sb, 1)
            for h in range(MLA_HEADS):
                act.wait_ge(s_q_ready, h + 1)
                act.activation(q_n[:, h, :], bank(h % 4)[:, 0:T], ACT.Copy)
                act.activation(q_r[0:64, h, :], bank(h % 4)[0:64, T:2 * T], ACT.Copy).then_inc(s_q_sb, 1)
            UNITS = 2 * MLA_HEADS
            for u in range(UNITS + 3):
                if u < UNITS:
                    act.wait_ge(s_m_ready, u + 1)
                    if u >= 3:
                        act.wait_ge(s_pt_ready, u - 2)
                    act.activation(probs[:, u % 3, :], bank(u % 3), ACT.Exp, bias=neg_max[:, u % 4:u % 4 + 1],
                                   scale=MLA_SCALE, accum_out=row_sum[:, u % 4:u % 4 + 1]).then_inc(s_exp_ready, 1)
                if 2 <= u < UNITS + 2:
                    v = u - 2
                    act.wait_ge(s_pt_ready, v + 1)
                    if v >= 3:
                        act.wait_ge(s_pv_ready, v - 2)
                    act.activation(probsT[:, v % 3, :, :].rearrange("p i q -> p (i q)"), bank(3 + v % 2), ACT.Copy
                                   ).then_inc(s_pt_sb, 1)
                if u >= 3 and (u - 3) % 2:
                    h = (u - 3) // 2
                    act.wait_ge(s_pv_ready, 2 * h + 2)
                    act.activation(o_T[:, h, :], bank(5 + h % 2)[:, 0:T], ACT.Copy).then_inc(s_o_sb, 1)

            norm(N_MOE, X, sq_moe, updated(X_FFN0), D)
            shift(N_MOE)
            for i in range(4):
                act.wait_ge(s_htok_t, i + 1)
                act.activation(h_hi[:, i // 2, 512 * (i % 2):512 * (i % 2) + 512], bank(1 + i), ACT.Copy).then_inc(s_htok_hi, 1)
            act.wait_ge(s_gap_ready, 1)
            act.activation(g2, gap, ACT.Exp).then_inc(s_gap_exp, 1)

            def tokens_hi(it):
                for b in range(2):
                    act.wait_ge(s_gather_ready, 2 * it + b + 1)
                    act.activation(x_hi[:, 4 * b:4 * b + 4, :].rearrange("p k s -> p (k s)"), bank(b), ACT.Copy).then_inc(s_xg_hi, 1)

            def expert(it):
                for q in range(QUARTERS):
                    j, r = divmod(q, 4)
                    if r == 0:
                        act.wait_ge(w_in[j % RING], expert_chunk_ready(it, j))
                    act.wait_ge(s_quarter_used, QUARTERS * it + q + 1)
                    act.activation(w_hi[:, q % SPLIT, :], ring[:, j % RING, r * QUARTER:(r + 1) * QUARTER], ACT.Copy
                                   ).then_inc(s_split_hi, 1)
                    if q == 5:
                        act.wait_ge(s_put_turned, it + 1)
                        act.activation(putT, bank(6)[:, 0:T], ACT.Copy).then_inc(s_put_sb, 1)
                    if r == 3 and 1 <= j <= UPS:
                        act.activation(e_silu[:, (j - 1) % 2, :], bank((j - 1) % 2)[:, 0:256], ACT.Silu).then_inc(s_up_silu, 1)
                    if r == 3 and 2 <= j <= UPS + 1:
                        act.wait_ge(s_ht_ready, UPS * it + j - 1)
                        act.activation(he_hi[:, 2 * j - 4:2 * j - 2, :].rearrange("p k s -> p (k s)"),
                                       bank(4 + j % 2)[:, 0:256], ACT.Copy).then_inc(s_he_hi, 1)
                act.wait_ge(s_quarter_used, QUARTERS * (it + 1) + SPLIT)
                act.activation(ye[:, 0:512], bank(6), ACT.Copy).then_inc(s_ye_sb, 1)
                tokens_hi(it + 1)

            act.wait_ge(s_items_ready, 1)
            tokens_hi(0)
            n_items = act.value_load(item_list[0:1, 3:4], min_val=N_EXPERTS, max_val=N_ITEMS)
            with act.Fori(0, n_items) as it:
                expert(it)

            norm(N_END1, X, sq_moe, updated(X_MIX1), D)
            norm(N_MIX2, X, sq_moe, lambda k: act.wait_ge(s_h_ready, tiles_before(N_END1) + k + 1), D)

            places = {"ka": ka, "va": va, "u": u_T, "qa": qa, "qm": qm, "km": km, "vm": vm, "gate": gates}

            def take(t):
                _, kind, _, (name, i) = PROJ[t]
                act.wait_ge(s_proj_ready, t + 1)
                src = bank(6 + t % 2)[:, 0:T]
                if kind == "tok":
                    a = act.activation(places[name].rearrange("p a b -> p (a b)"), src, ACT.Copy)
                else:
                    a = act.activation(places[name][:, i, :], src, ACT.Sigmoid if name == "gate" else ACT.Copy)
                a.then_inc(s_proj_sb, 1)

            def soft(a):
                act.wait_ge(s_am_ready, a + 1)
                for i, (lo, hi) in enumerate(((0, P), (P, 384))):
                    x = act.activation(p2[:, a % 2, lo:hi], p2[:, a % 2, lo:hi], ACT.Exp, bias=a_neg[:, a % 2, i:i + 1],
                                       scale=SCALE2, accum_out=a_sum[:, a % 2, i:i + 1])
                if a < 8:
                    x = act.activation(a_sink[:, a % 2, :], a_neg[:, a % 2, :], ACT.Exp, bias=pr("sinks")[:, a:a + 1])
                x.then_inc(s_ae_ready, 1)

            def take_turned(a):
                act.wait_ge(s_apt_ready, a + 1)
                if a >= 2:
                    act.wait_ge(s_ao_ready, a - 1)
                act.activation(pT2[:, a % 2, :], bank(2)[:, 0:384], ACT.Copy).then_inc(s_apt_sb, 1)

            for t in CHUNK_ITEMS[C2_A] + CHUNK_ITEMS[C2_B]:
                take(t)
            for i in range(8):
                act.wait_ge(s_bb_t, i + 1)
                v, k = divmod(4 * i, SSM_TILES)
                a = act.activation(bb_T[:, v, k:k + 4, :].rearrange("p k s -> p (k s)"), bank(i % 4), ACT.Copy)
                a.then_inc(s_bb_sb, 1)
            for r in range(ROUNDS + 1):
                items = round_items(r)
                if items:
                    take(items[0])
                if r >= 2 and r % 2 == 0:
                    j = r // 2 - 1
                    act.wait_ge(s_y_psum, j + 1)
                    act.activation(u_T[:, j, :], bank(3)[:, T:2 * T], ACT.Gelu_apprx_tanh).then_inc(s_y_sb, 1)
                if items:
                    take(items[1])
                if r:
                    soft(2 * r - 2)
                    soft(2 * r - 1)
                for t in items[2:3]:
                    take(t)
                if r:
                    take_turned(2 * r - 2)
                for t in items[3:]:
                    take(t)
                if r:
                    take_turned(2 * r - 1)
                    act.wait_ge(s_ao_ready, 2 * r)
                    dst = qa if r <= 4 else qm
                    act.activation(dst[:, (r - 1) % 4, :], bank(3)[:, 0:T], ACT.Copy).then_inc(s_ao_sb, 1)
            for i in range(4):
                act.wait_ge(s_br_ready, 16 + 2 * i + 1)
                if i >= 2:
                    act.wait_ge(s_br_free, 16 + 2 * (i - 1))
                act.activation(glu_s[:, i % 2, :], bank((16 + 2 * i) % 8)[:, 0:T], ACT.Sigmoid).then_inc(s_glu_sig, 1)
            norm(N_FFN2, X, sq2, updated(X_MOE), D)

            def relu(at, i):
                act.wait_ge(s_ff1_ready, at + 1)
                act.activation(ff_relu[:, i % 6, :], bank(i % 6)[:, 0:T], ACT.Relu).then_inc(s_ff1_relu, 1)

            with act.Fori(0, 2) as g:
                for i in range(12):
                    relu(12 * g + i, i)
            for i in range(24, 32):
                relu(i, i)
            norm(N_END2, X, sq2, updated(X_MIX2), D)

        @block.vector
        def _(dve):
            def norm(n, src, dst, g, signal):
                kt, sets, _ = NORMS[n]
                dve.wait_ge(s_norm_std, n + 1)
                r = rstd[:, n % 2, 0:sets * T]
                dve.reciprocal(r, r)
                dve.drain()
                for k in range(kt):
                    for s in range(sets):
                        i = dve.scalar_tensor_tensor(dst[:, s, k, :], src[:, s, k, :], g(k, s), r[:, s * T:(s + 1) * T],
                                                     ALU.mult, ALU.mult)
                    i.then_inc(signal, 1)

            def modulated(n):
                layer, at = norm_place(n)
                norm(n, X, H, lambda k, s: gain[:, 2 * layer + at // 24, k, s:s + 1], s_norm_scaled)

            def column(name):
                return lambda k, s: pr(name)[:, k:k + 1]

            def add_gated(dst_tile, ready, count, b, layer, at, sets):
                dve.wait_ge(ready, count)
                for s in range(sets):
                    x = X[:, s, dst_tile, :]
                    i = dve.scalar_tensor_tensor(x, bank2(b)[:, s, :], mod[:, layer, at + dst_tile, s:s + 1], x, ALU.mult, ALU.add)
                i.then_inc(s_x_updated, 1)

            def modulation(layer):
                dve.wait_ge(s_ada_cols, 12 * (layer + 1))
                b = pr("b_ada")[:, 48 * layer:48 * layer + 48]
                dve.tensor_tensor(mod[:, layer, :, :], psum[:, 2, 0:96].rearrange("p (v s) -> p v s", s=2),
                                  b.unsqueeze(2).broadcast_to([P, 48, 2]), ALU.add).then_inc(s_mod_ready, 1)
                dve.drain()
                for w in range(2):
                    i = 2 * layer + w
                    g = pr("norm_g")[:, 8 * i:8 * i + 8]
                    dve.scalar_tensor_tensor(gain[:, i, :, :], mod[:, layer, 24 * w + 8:24 * w + 16, :], 1.0,
                                             g.unsqueeze(2).broadcast_to([P, KT, 2]), ALU.add, ALU.mult)
                dve.drain()

            dve.memset(ones[:, :], 1.0).then_inc(s_ones_ready, 1)
            dve.sem_inc(s_ffn_free, 3)
            dve.sem_inc(s_eh_ready, 2)
            dve.sem_inc(s_he_ready, 2)
            dve.sem_inc(s_ff1_free, 6)

            dve.wait_ge(s_small_in, 32)
            lr, li = pr("lam_re"), pr("lam_im")
            sc = [scr[:, i, :] for i in range(10)]
            dve.wait_ge(s_ssm_theta, 1)
            dve.tensor_tensor(sc[1], lr, sc[0], ALU.mult).then_inc(s_ssm_theta2, 1)
            dve.tensor_tensor(sc[4], li, sc[0], ALU.mult)
            dve.drain()
            magic = 1.5 * 2.0 ** 23
            dve.tensor_scalar(sc[5], sc[4], 1.0 / (2 * np.pi), magic, ALU.mult, ALU.add)
            dve.drain()
            dve.tensor_scalar(sc[5], sc[5], magic, None, ALU.subtract)
            two_pi = [6.28125, 0.00193500518798828125, 2 * np.pi - 6.28125 - 0.00193500518798828125]
            for part in two_pi:
                dve.drain()
                dve.scalar_tensor_tensor(sc[4], sc[5], -part, sc[4], ALU.mult, ALU.add)
            dve.drain()
            dve.tensor_scalar(sc[2], sc[4], 3.1415925, -3.1415925, ALU.min, ALU.max).then_inc(s_ssm_theta2, 1)
            dve.wait_ge(s_ssm_sin, 2)
            dve.tensor_tensor(sc[5], sc[3], sc[3], ALU.mult)
            dve.tensor_tensor(sc[6], mag, sin1, ALU.mult)
            dve.tensor_tensor(sc[8], lr, lr, ALU.mult)
            dve.tensor_tensor(sc[9], li, li, ALU.mult)
            dve.drain()
            dve.tensor_scalar(cos1, sc[5], -2.0, 1.0, ALU.mult, ALU.add)
            dve.tensor_tensor(sc[8], sc[8], sc[9], ALU.add)
            dve.drain()
            dve.tensor_tensor(sc[7], mag, cos1, ALU.mult)
            dve.reciprocal(sc[8], sc[8])
            dve.drain()
            dve.tensor_scalar(sc[7], sc[7], 1.0, None, ALU.subtract)
            dve.drain()
            dve.tensor_tensor(sc[0], sc[7], lr, ALU.mult)
            dve.tensor_tensor(sc[1], sc[6], li, ALU.mult)
            dve.tensor_tensor(sc[4], sc[6], lr, ALU.mult)
            dve.tensor_tensor(sc[5], sc[7], li, ALU.mult)
            dve.drain()
            dve.tensor_tensor(sc[0], sc[0], sc[1], ALU.add)
            dve.tensor_tensor(sc[4], sc[4], sc[5], ALU.subtract)
            dve.drain()
            dve.tensor_tensor(f_re, sc[0], sc[8], ALU.mult)
            dve.tensor_tensor(f_im, sc[4], sc[8], ALU.mult).then_inc(s_ssm_f, 1)

            modulation(0)
            modulated(N_MIX0)
            dve.wait_ge(s_pad_zero, 1)
            for i in range(4):
                dve.wait_ge(s_sig_ready, i + 1)
                dve.tensor_tensor(apad[:, i, :, PAD:PAD + T], bank2(i), sig[:, i, :].rearrange("p (s t) -> p s t", s=2),
                                  ALU.mult).then_inc(s_a_ready, 1)
            for i in range(4):
                dve.wait_ge(s_v_act, i + 1)
                dve.bn_stats(v_stats[:, i, :], vln[:, i, :])
            dve.drain()
            for i in range(4):
                a = dve.bn_aggr(v_mv[:, i, :], v_stats[:, i, :])
            a.then_inc(s_v_var, 1)
            dve.wait_ge(s_v_std, 1)
            dve.reciprocal(v_rs, v_rs)
            dve.drain()
            for i in range(4):
                dve.tensor_scalar(vln[:, i, :], vln[:, i, :], v_mv[:, i, 0:1], v_rs[:, i:i + 1], ALU.subtract, ALU.mult)
            dve.drain()
            dve.wait_ge(s_mixer_in, 16)
            dve.tensor_tensor(vln, vln, ln_v_g.unsqueeze(1).broadcast_to([P, 4, 512]), ALU.mult)
            dve.drain()
            dve.tensor_tensor(vln, vln, ln_v_b.unsqueeze(1).broadcast_to([P, 4, 512]), ALU.add).then_inc(s_v_ln, 4)
            taps = pr("conv_w").rearrange("p (i k) -> p i k", i=4)
            conv = [cat[:, i, :].rearrange("p (s t) -> p s t", s=2) for i in range(4)]
            for i in range(4):
                dve.tensor_scalar(conv[i], apad[:, i, :, 0:T], taps[:, i, 0:1], pr("conv_b")[:, i:i + 1], ALU.mult, ALU.add)
            dve.drain()
            with dve.Fori(1, CONV_K - 1) as k:
                for i in range(4):
                    dve.scalar_tensor_tensor(conv[i], apad[:, i, :, bass.ds(k, T)], taps[:, i, bass.ds(k, 1)], conv[i],
                                             ALU.mult, ALU.add)
                dve.drain()
            for i in range(4):
                dve.scalar_tensor_tensor(conv[i], apad[:, i, :, CONV_K - 1:CONV_K - 1 + T], taps[:, i, CONV_K - 1:CONV_K],
                                         conv[i], ALU.mult, ALU.add).then_inc(s_conv_ready, 1)
            dve.wait_ge(s_u_act, 4)
            for j in range(4):
                dve.wait_ge(s_sgu_ready, j + 1)
                dve.tensor_tensor(sig[:, j, :].rearrange("p (n t) -> p n t", n=4), bank(4 + j).rearrange("p (n t) -> p n t", n=4),
                                  b_s[:, j, :].unsqueeze(1).broadcast_to([P, 4, P]), ALU.add)
            dve.drain()
            for j in range(4):
                dve.tensor_tensor(cat[:, 4 + j, :], cat[:, 4 + j, :], sig[:, j, :], ALU.mult).then_inc(s_bo_ready, 1)
            modulation(1)
            dve.wait_ge(s_lna_mean, 1)
            for i in range(4):
                dve.tensor_tensor(cat[:, i, :], cat[:, i, :], rstd[:, 1, :], ALU.subtract).then_inc(s_lna_centered, 1)
            dve.wait_ge(s_lna_std, 1)
            dve.reciprocal(rstd[:, 0, :], rstd[:, 0, :])
            dve.drain()
            for i in range(4):
                dve.tensor_tensor(cat[:, i, :], cat[:, i, :], rstd[:, 0, :], ALU.mult).then_inc(s_lna_scaled, 1)
            for i in range(KT):
                add_gated(i, s_mix_ready, i + 1, i, 0, 16, 2)

            modulated(N_FFN0)

            def ffn_product(at, i):
                dve.wait_ge(s_ffn_silu, at + 1)
                dve.wait_ge(s_ffn_up, 2 * at + 2)
                dve.tensor_tensor(ffn_h[:, bass.ds(at, 1), :].rearrange("p a t -> p (a t)"), ffn_s[:, i % 3, :],
                                  bank(2 * (i % 3) + 1), ALU.mult).then_inc(s_ffn_free, 1)

            with dve.Fori(0, 3) as g:
                for i in range(6):
                    ffn_product(6 * g + i, i)
            for i in range(18, FT):
                ffn_product(i, i)
            for i in range(KT):
                add_gated(i, s_ffn_down, 3 * (i // 4 + 1), i, 0, 40, 2)

            modulated(N_MIX1)
            norm(N_KV, kv_lat, kv_lat, column("g_kv"), s_h_ready)
            norm(N_Q, q_lat, q_lat, column("g_q"), s_h_ready)
            cos, sin = cn("cos")[0:64, :], cn("sin")[0:64, :]
            dve.wait_ge(s_rot_ready, 1)
            dve.tensor_tensor(rot_t[0:64, 0, :], psum[0:64, 2, 0:T], sin, ALU.mult)
            dve.tensor_tensor(k_pe[0:64, 0, :], k_pe[0:64, 0, :], cos, ALU.mult)
            dve.drain()
            dve.tensor_tensor(k_pe[0:64, 0, :], k_pe[0:64, 0, :], rot_t[0:64, 0, :], ALU.add).then_inc(s_kpe_ready, 1)
            for i in range(8):
                dve.wait_ge(s_v_ready, i + 1)
                dve.tensor_copy(v_tok[:, i // 2, 512 * (i % 2):512 * (i % 2) + 512], bank(4 + i % 3)).then_inc(s_v_sb, 1)
            for i in range(4):
                dve.wait_ge(s_rot_ready, i + 2)
                pair = slice(2 * i, 2 * i + 2)
                dve.tensor_tensor(rot_t[0:64, pair, :], bank2(4 + i % 3)[0:64], sin.unsqueeze(1).broadcast_to([64, 2, T]), ALU.mult)
                dve.tensor_tensor(q_r[0:64, pair, :], q_r[0:64, pair, :], cos.unsqueeze(1).broadcast_to([64, 2, T]), ALU.mult)
                dve.drain()
                dve.tensor_tensor(q_r[0:64, pair, :], q_r[0:64, pair, :], rot_t[0:64, pair, :], ALU.add).then_inc(s_qr_ready, 1)
            UNITS = 2 * MLA_HEADS
            for u in range(UNITS + 1):
                if u < UNITS:
                    c = slice(u % 4, u % 4 + 1)
                    dve.wait_ge(s_s_ready, u + 1)
                    dve.reduce_max(row_max[:, c], bank(u % 3), AX)
                    dve.drain()
                    dve.tensor_scalar(neg_max[:, c], row_max[:, c], -MLA_SCALE, None, ALU.mult).then_inc(s_m_ready, 1)
                if u:
                    v = u - 1
                    c = slice(v % 4, v % 4 + 1)
                    dve.wait_ge(s_exp_ready, v + 1)
                    dve.reciprocal(row_sum[:, c], row_sum[:, c])
                    dve.drain()
                    dve.tensor_scalar(probs[:, v % 3, :], probs[:, v % 3, :], row_sum[:, c], None, ALU.mult).then_inc(s_p_ready, 1)
            for i in range(KT):
                add_gated(i, s_wo_ready, i + 1, i, 1, 16, 1)

            modulated(N_MOE)
            iota8 = cn("iota8").unsqueeze(1).broadcast_to([P, 2, 8])

            def wide(col):
                return col.unsqueeze(2).broadcast_to([P, 2, 8])

            def choose(values, top, chosen):
                dve.tensor_reduce(top, values, AX, ALU.max)
                dve.drain()
                dve.tensor_tensor(eq8, values, wide(top), ALU.is_equal)
                dve.drain()
                dve.scalar_tensor_tensor(eq8, eq8, -8.0, iota8, ALU.mult, ALU.add)
                dve.drain()
                dve.tensor_reduce(where1, eq8, AX, ALU.min)
                dve.drain()
                dve.tensor_scalar(where1, where1, 8.0, None, ALU.add)
                dve.drain()
                dve.tensor_tensor(chosen, iota8, wide(where1), ALU.is_equal)
                dve.drain()

            dve.wait_ge(s_logits_ready, 1)
            dve.tensor_copy(logits, bank(0)[:, 0:16].rearrange("p (t e) -> p t e", t=2))
            dve.drain()
            choose(logits, top1, first8)
            dve.scalar_tensor_tensor(work8, first8, -1e30, logits, ALU.mult, ALU.add)
            dve.drain()
            choose(work8, top2, second8)
            dve.tensor_tensor(mask8, first8, second8, ALU.add)
            dve.tensor_tensor(gap, top2, top1, ALU.subtract).then_inc(s_gap_ready, 1)
            dve.drain()
            dve.sem_inc(s_masks_ready, 1)
            dve.wait_ge(s_gap_exp, 1)
            dve.tensor_scalar(g1, g2, 1.0, None, ALU.add)
            dve.drain()
            dve.reciprocal(g1, g1)
            dve.drain()
            dve.tensor_tensor(g2, g2, g1, ALU.mult)
            dve.drain()
            dve.tensor_tensor(gate8, first8, wide(g1), ALU.mult)
            dve.tensor_tensor(work8, second8, wide(g2), ALU.mult)
            dve.drain()
            dve.tensor_tensor(gate8, gate8, work8, ALU.add)
            dve.wait_ge(s_rank_ready, 1)
            dve.tensor_copy(rank8, bank(5)[:, 0:16].rearrange("p (t e) -> p t e", t=2))
            dve.tensor_scalar(over8, bank(5)[:, 16:24], float(P), None, ALU.is_gt)
            dve.drain()
            dve.tensor_tensor_scan(place8, ones[:, 0:8], over8, 0.0, ALU.mult, ALU.add)
            for table, own in ((item_rank, rank8), (item_mask, mask8), (item_gate, gate8)):
                dve.tensor_copy(table[:, :, 0:N_EXPERTS], own)
            dve.drain()
            dve.tensor_scalar(chosen_f[:, 3:4], place8[:, 7:8], float(N_EXPERTS), None, ALU.add)
            for s in range(SPARE):
                dve.scalar_tensor_tensor(eq8[:, 0, :], place8, float(s + 1), over8, ALU.is_equal, ALU.mult)
                dve.drain()
                dve.tensor_tensor(eq8[:, 1, :], eq8[:, 0, :], cn("iota8"), ALU.mult)
                dve.drain()
                dve.tensor_reduce(chosen_f[:, s:s + 1], eq8[:, 1, :], AX, ALU.add)
                for table, own in ((item_rank, rank8), (item_mask, mask8), (item_gate, gate8)):
                    dve.drain()
                    dve.tensor_tensor(work8, own, eq8[:, 0:1, :].broadcast_to([P, 2, 8]), ALU.mult)
                    dve.drain()
                    dve.tensor_reduce(table[:, :, N_EXPERTS + s], work8, AX, ALU.add)
                dve.drain()
            spare = slice(N_EXPERTS, N_ITEMS)
            dve.tensor_scalar(item_rank[:, :, spare], item_rank[:, :, spare], float(P), None, ALU.subtract)
            for table in (item_rank, item_mask, item_gate):
                dve.memset(table[:, :, N_ITEMS], 0.0)
            dve.tensor_copy(item_list[:, :], chosen_f).then_inc(s_items_ready, 1)
            dve.tensor_scalar(sink8, pr("sinks"), 1.0 / SCALE2, None, ALU.mult)
            dve.wait_ge(s_items_ready, 1)
            dve.drain()

            def select(it):
                for t in range(2):
                    rank, m, g = (v[:, t, bass.ds(it, 1)] for v in (item_rank, item_mask, item_gate))
                    dve.tensor_scalar(pick[:, t, :], cn("iota"), rank, m, ALU.is_equal, ALU.mult)
                    x = dve.tensor_scalar(put[:, t, :], cn("iota"), rank, g, ALU.is_equal, ALU.mult)
                x.then_inc(s_select_ready, 1)

            def tokens_lo(it):
                for b in range(2):
                    k = slice(4 * b, 4 * b + 4)
                    dve.wait_ge(s_xg_hi, 2 * it + b + 1)
                    dve.tensor_tensor(x_lo[:, k, :].rearrange("p k s -> p (k s)"), bank(b),
                                      x_hi[:, k, :].rearrange("p k s -> p (k s)").bitcast(F32), ALU.subtract).then_inc(s_xg_ready, 1)

            def add_y(it, b):
                y = y_T[:, 2 * b:2 * b + 2, :]
                if b == 0:
                    dve.wait_ge(s_y_ready, 4 * it + 4)
                dve.tensor_tensor(y, y, bank2(2 + b), ALU.add).then_inc(s_y_added, 1)

            def expert(it):
                for q in range(QUARTERS):
                    j, r = divmod(q, 4)
                    dve.wait_ge(s_split_hi, QUARTERS * it + q + 1)
                    dve.tensor_tensor(w_lo[:, q % SPLIT, :], ring[:, j % RING, r * QUARTER:(r + 1) * QUARTER],
                                      w_hi[:, q % SPLIT, :].bitcast(F32), ALU.subtract).then_inc(s_split_lo, 1)
                    if r == 3 and 1 <= j <= UPS:
                        i = j - 1
                        dve.wait_ge(s_up_silu, UPS * it + i + 1)
                        dve.tensor_tensor(e_h[:, i % 2, :], e_silu[:, i % 2, :], bank(i % 2)[:, 256:512], ALU.mult
                                          ).then_inc(s_eh_ready, 1)
                    if r == 3 and 2 <= j <= UPS + 1:
                        k = slice(2 * j - 4, 2 * j - 2)
                        dve.wait_ge(s_he_hi, UPS * it + j - 1)
                        dve.tensor_tensor(he_lo[:, k, :].rearrange("p k s -> p (k s)"), bank(4 + j % 2)[:, 0:256],
                                          he_hi[:, k, :].rearrange("p k s -> p (k s)").bitcast(F32), ALU.subtract
                                          ).then_inc(s_he_ready, 1)
                    if 2 <= q < 6:
                        add_y(it, q - 2)
                    if q == UP_QUARTERS:
                        select(it + 1)
                dve.wait_ge(s_quarter_used, QUARTERS * (it + 1) + SPLIT)
                dve.tensor_copy(ye[:, 512:1024], bank(7)).then_inc(s_ye_sb, 1)
                tokens_lo(it + 1)

            dve.wait_ge(s_e_ready, 1)
            select(0)
            for i in range(4):
                v = slice(512 * (i % 2), 512 * (i % 2) + 512)
                dve.wait_ge(s_htok_hi, i + 1)
                dve.tensor_tensor(h_lo[:, i // 2, v], bank(1 + i), h_hi[:, i // 2, v].bitcast(F32), ALU.subtract).then_inc(s_htok_sb, 1)
            tokens_lo(0)
            n_items = dve.value_load(item_list[0:1, 3:4], min_val=N_EXPERTS, max_val=N_ITEMS)
            with dve.Fori(0, n_items) as it:
                expert(it)
            for b in range(4):
                add_y(n_items, b)
            dve.drain()
            for i in range(KT):
                x = X[:, 0, i, :]
                dve.scalar_tensor_tensor(x, y_T[:, i, :], mod[:, 1, 40 + i, 0:1], x, ALU.mult, ALU.add).then_inc(s_x_updated, 1)

            norm(N_END1, X, X, column("final_g"), s_h_ready)
            norm(N_MIX2, X, H, column("norm_mix"), s_h_ready)
            for j in range(4):
                x = dve.tensor_scalar(diag_d[:, j, :], ident, pr("d_skip")[:, j:j + 1], None, ALU.mult)
            x.then_inc(s_diag_ready, 1)

            def turns(tab, r, chunks):
                t = tab[:, 2 * r:2 * r + 2, :]
                return t.unsqueeze(2).broadcast_to([P, 2, 2, SSM_L]) if chunks else t

            def by_chunk(v):
                return v.rearrange("p i (c t) -> p i c t", c=2)

            def state_drive(r):
                er, ei = turns(rot_re, r, True), turns(rot_im, r, True)
                xr, xi = by_chunk(bank2(4)), by_chunk(bank2(5))
                t0, t1 = by_chunk(ssm_t[:, 0]), by_chunk(ssm_t[:, 1])
                dve.wait_ge(s_xs_ready, r + 1)
                dve.tensor_tensor(t0, er, xr, ALU.mult)
                dve.tensor_tensor(t1, ei, xi, ALU.mult)
                dve.drain()
                dve.tensor_tensor(ssm_w[:, 0], ssm_t[:, 0], ssm_t[:, 1], ALU.add)
                dve.drain()
                dve.tensor_tensor(t0, er, xi, ALU.mult)
                dve.tensor_tensor(t1, ei, xr, ALU.mult).then_inc(s_xs_used, 1)
                dve.drain()
                dve.tensor_tensor(ssm_w[:, 1], ssm_t[:, 0], ssm_t[:, 1], ALU.subtract)
                dve.drain()

            def state_scan(r, c):
                at = slice(c * SSM_L, (c + 1) * SSM_L)
                tiles = [(2 * r + i) % 4 for i in range(2)]
                for i in range(2):
                    decay = mag[:, 2 * r + i:2 * r + i + 1].broadcast_to([P, SSM_L])
                    for v in range(2):
                        w = ssm_w[:, v, i, at]
                        start = ssm_h[:, v, tiles[i], c * SSM_L - 1:c * SSM_L] if c else 0.0
                        dve.tensor_tensor_scan(w, decay, w, start, ALU.mult, ALU.add)
                dve.drain()
                if c == 0 and r >= 2 and r % 2 == 0:
                    dve.wait_ge(s_y_psum, r // 2)
                er, ei = turns(rot_re, r, False), turns(rot_im, r, False)
                t0, t1 = ssm_t[:, 0, :, 0:SSM_L], ssm_t[:, 1, :, 0:SSM_L]
                h = [ssm_h[:, v, tiles[0]:tiles[0] + 2, at] for v in range(2)]
                dve.tensor_tensor(t0, er, ssm_w[:, 0, :, at], ALU.mult)
                dve.tensor_tensor(t1, ei, ssm_w[:, 1, :, at], ALU.mult)
                dve.drain()
                dve.tensor_tensor(h[0], t0, t1, ALU.subtract)
                dve.drain()
                dve.tensor_tensor(t0, er, ssm_w[:, 1, :, at], ALU.mult)
                dve.tensor_tensor(t1, ei, ssm_w[:, 0, :, at], ALU.mult)
                dve.drain()
                dve.tensor_tensor(h[1], t0, t1, ALU.add).then_inc(s_hs_ready, 1)
                dve.drain()

            def biased(a):
                s = a % 2
                dve.wait_ge(s_as_ready, a + 1)
                if a >= 2:
                    dve.wait_ge(s_apt_ready, a - 1)
                dist = cn("swa_dist") if a < 8 else cn("moba_dist")
                dve.scalar_tensor_tensor(p2[:, s, :], dist, -float(SLOPES[a]) / SCALE2, bank(s)[:, 0:384], ALU.mult, ALU.add)
                dve.drain()
                dve.reduce_max(a_max[:, s, 0:1], p2[:, s, 0:P], AX)
                dve.reduce_max(a_max[:, s, 1:2], p2[:, s, P:384], AX)
                dve.drain()
                if a < 8:
                    i = dve.tensor_scalar(a_neg[:, s, :], a_max[:, s, :], sink8[:, a:a + 1], -SCALE2, ALU.max, ALU.mult)
                else:
                    i = dve.tensor_scalar(a_neg[:, s, :], a_max[:, s, :], -SCALE2, None, ALU.mult)
                i.then_inc(s_am_ready, 1)

            def normalised(a):
                s = a % 2
                dve.wait_ge(s_ae_ready, a + 1)
                if a < 8:
                    dve.tensor_tensor(a_sum[:, s, :], a_sum[:, s, :], a_sink[:, s, :], ALU.add)
                    dve.drain()
                dve.reciprocal(a_sum[:, s, :], a_sum[:, s, :])
                dve.drain()
                dve.tensor_scalar(p2[:, s, 0:P], p2[:, s, 0:P], a_sum[:, s, 0:1], None, ALU.mult)
                dve.tensor_scalar(p2[:, s, P:384], p2[:, s, P:384], a_sum[:, s, 1:2], None, ALU.mult).then_inc(s_ap_ready, 1)

            dve.wait_ge(s_e_ready, 1)
            for r in range(ROUNDS + 1):
                if r < ROUNDS:
                    state_drive(r)
                if r:
                    biased(2 * r - 2)
                    biased(2 * r - 1)
                if r < ROUNDS:
                    state_scan(r, 0)
                if r:
                    normalised(2 * r - 2)
                    normalised(2 * r - 1)
                if r < ROUNDS:
                    state_scan(r, 1)

            dve.wait_ge(s_proj_sb, len(PROJ))
            for g in range(8):
                dve.wait_ge(s_br_ready, g + 1)
                dve.tensor_tensor(mixed[:, g, :], bank(g)[:, 0:T], gates[:, g, :], ALU.mult).then_inc(s_br_free, 1)

            def add_branch(g, gate0):
                i = g % 8
                dve.wait_ge(s_br_ready, g + 1)
                dve.tensor_tensor(mix_t[:, i % 2, :], bank(i)[:, 0:T], gates[:, gate0 + i, :], ALU.mult)
                dve.drain()
                dve.tensor_tensor(mixed[:, i, :], mixed[:, i, :], mix_t[:, i % 2, :], ALU.add).then_inc(s_br_free, 1)

            for g in range(8, 16):
                add_branch(g, 16)
            for i in range(4):
                dve.wait_ge(s_glu_sig, i + 1)
                dve.wait_ge(s_br_ready, 16 + 2 * i + 2)
                dve.tensor_tensor(glu_z[:, i, :], bank((17 + 2 * i) % 8)[:, 0:T], glu_s[:, i % 2, :], ALU.mult).then_inc(s_br_free, 2)
            for g in range(24, 32):
                add_branch(g, 8)

            def add_bank(i, ready, count):
                dve.wait_ge(ready, count)
                dve.tensor_tensor(X[:, 0, i, :], X[:, 0, i, :], bank(i)[:, 0:T], ALU.add).then_inc(s_x_updated, 1)

            for i in range(KT):
                add_bank(i, s_wout_ready, i + 1)
            norm(N_FFN2, X, H, column("norm_ffn"), s_h_ready)

            def squared(at, i):
                dve.wait_ge(s_ff1_relu, at + 1)
                dve.tensor_tensor(ff_h[:, bass.ds(at, 1), :].rearrange("p a t -> p (a t)"), ff_relu[:, i % 6, :],
                                  bank(i % 6)[:, 0:T], ALU.mult).then_inc(s_ff1_free, 1)

            with dve.Fori(0, 2) as g:
                for i in range(12):
                    squared(12 * g + i, i)
            for i in range(24, 32):
                squared(i, i)
            for i in range(KT):
                add_bank(i, s_ff2_used, 8)
            norm(N_END2, X, H, column("norm_final"), s_h_ready)

        @block.gpsimd
        def _(pool):
            pool.memset(apad, 0.0).then_inc(s_pad_zero, 1)
            pool.wait_ge(s_ssm_f, 1)
            pool.wait_ge(s_lat_ready, 6)
            pool.tensor_copy(rot_re[:, :, 0], cos1)
            pool.tensor_copy(rot_im[:, :, 0], sin1)
            n = 1
            while n < SSM_L:
                pool.drain()
                ar, ai = rot_re[:, :, 0:n], rot_im[:, :, 0:n]
                br, bi = (t[:, :, n - 1:n].broadcast_to([P, SSM_TILES, n]) for t in (rot_re, rot_im))
                ta, tb = (t[:, 0:SSM_TILES * n].rearrange("p (i t) -> p i t", i=SSM_TILES) for t in (tmp_a, tmp_b))
                pool.tensor_tensor(ta, ar, br, ALU.mult)
                pool.tensor_tensor(tb, ai, bi, ALU.mult)
                pool.drain()
                pool.tensor_tensor(rot_re[:, :, n:2 * n], ta, tb, ALU.subtract)
                pool.drain()
                pool.tensor_tensor(ta, ar, bi, ALU.mult)
                pool.tensor_tensor(tb, ai, br, ALU.mult)
                pool.drain()
                pool.tensor_tensor(rot_im[:, :, n:2 * n], ta, tb, ALU.add)
                n *= 2
            pool.drain()
            pool.sem_inc(s_e_ready, 1)
            pool.wait_ge(s_x_updated, X_MIX1)
            pool.memset(y_T, 0.0).then_inc(s_y_zero, 1)
            pool.wait_ge(s_x_updated, X_MOE)
            pool.dma_start(ssm_raw, A["ssm"].rearrange("p (m i h) -> p m i h", m=4, i=SSM_TILES)).then_inc(s_ssm_in, 16)
            for v in range(2):
                pool.memset(b_wide[:, v, :, :], 0.0)
                pool.memset(c_wide[:, v, :, :], 0.0)
            pool.wait_ge(s_ssm_in, 16)
            quarter = [b_part[:, i] for i in range(4)]
            fr, fi = (f.unsqueeze(2).broadcast_to([P, SSM_TILES, 16]) for f in (f_re, f_im))
            b_re, b_im = ssm_raw[:, 0], ssm_raw[:, 1]
            pool.tensor_tensor(quarter[0], b_re, fr, ALU.mult)
            pool.tensor_tensor(quarter[1], b_im, fi, ALU.mult)
            pool.drain()
            pool.tensor_tensor(quarter[2], quarter[0], quarter[1], ALU.subtract)
            pool.drain()
            pool.tensor_tensor(quarter[0], b_im, fr, ALU.mult)
            pool.tensor_tensor(quarter[1], b_re, fi, ALU.mult)
            pool.drain()
            pool.tensor_tensor(quarter[3], quarter[0], quarter[1], ALU.add)
            pool.drain()
            for half in range(2):
                rows = slice(64 * half, 64 * half + 64)
                for q in range(4):
                    c = slice(32 * q + 16 * half, 32 * q + 16 * half + 16)
                    for v in range(2):
                        pool.tensor_copy(b_wide[rows, v, q::4, c], quarter[2 + v][rows, q::4, :])
                        pool.tensor_scalar(c_wide[rows, v, q::4, c], ssm_raw[rows, 2 + v, q::4, :], 1.0 - 2.0 * v, None, ALU.mult)
            pool.drain()
            pool.sem_inc(s_ssm_expanded, 1)


_WEIGHTS = ["w_ada", "e_w_in", "e_w_out", "e_ffn_w1", "e_ffn_w3", "e_ffn_w2", "o_w_in", "o_w_uq", "o_w_ukv", "o_w_o",
            "o_exp_w1", "o_exp_w3", "o_exp_w2", "w_in_2", "w_glu_2", "w_o_swa_2", "w_o_ssm_2", "w_o_moba_2", "w_out_2",
            "w_ff1_2", "w_ff2_2"]


def constants():
    f = np.float32
    out = np.zeros((P, N_CONST), f)

    def put(name, v):
        a, _ = CONST_COLS[name]
        out[0:v.shape[0], a:a + v.shape[1]] = v

    put("ident", np.eye(P, dtype=f))
    put("tri", np.triu(np.ones((P, P), f), 1))
    put("iota", np.broadcast_to(np.arange(P, dtype=f), (P, P)))
    put("iota8", np.broadcast_to(np.arange(8, dtype=f), (P, 8)))
    q, k = np.arange(T)[:, None], np.arange(T)[None, :]
    dist = (q - k).astype(f)
    for name, seen in (("swa_dist", (dist >= 0) & (dist < SWA_WINDOW)), ("moba_dist", dist >= 0)):
        d = np.where(seen, dist, f(FAR)).astype(f)
        put(name, np.concatenate([d[0:P, 0:P], d[P:T, :]], axis=1))
    rot = np.zeros((ROPE, ROPE), f)
    for m in range(ROPE):
        rot[(m + 16, m) if m % 32 < 16 else (m - 16, m)] = -1.0 if m % 32 < 16 else 1.0
    put("rot", rot)
    inv = f(10000.0) ** (-np.arange(16, dtype=f) / f(16))
    t = np.arange(T)
    pos = np.stack([t // 64, t % 64]).astype(f)
    ang = np.stack([pos[d // 32] * inv[d % 16] for d in range(ROPE)]).astype(f)
    put("cos", np.cos(ang))
    put("sin", np.sin(ang))
    return out


def pack(v):
    def tiles(a):
        return np.asarray(a).reshape(-1, P).T

    def states(a):
        a = np.asarray(a)
        a = a.reshape((16, 2, 64) + a.shape[2:])
        return np.moveaxis(a, 0, 2).reshape((P, 16) + a.shape[3:])

    c = np.stack([tiles(v["c"]), tiles(v["c_ctx"])], axis=2).reshape(P, 16)
    conv = np.asarray(v["e_conv_w"])[0].reshape(CONV_K, 4, P).transpose(2, 1, 0).reshape(P, 4 * CONV_K)
    step = np.repeat(np.asarray(v["log_step_2"])[0].reshape(16, 2).T, 64, axis=0)
    cols = {"c": c, "norm_g": tiles(v["norm_g"]), "b_ada": tiles(v["b_ada"]), "final_g": tiles(v["final_g"]),
            "norm_mix": tiles(v["norm_mix_2"]), "norm_ffn": tiles(v["norm_ffn_2"]), "norm_final": tiles(v["norm_final_2"]),
            "conv_b": tiles(v["e_conv_b"]), "ln_a_g": tiles(v["e_ln_a_g"]), "ln_a_b": tiles(v["e_ln_a_b"]),
            "d_skip": tiles(v["d_skip_2"]), "g_q": tiles(v["o_g_q"]), "g_kv": tiles(v["o_g_kv"]), "conv_w": conv,
            "lam_re": states(v["lam_re_2"][0]), "lam_im": states(v["lam_im_2"][0]), "log_step": step,
            "sinks": np.broadcast_to(np.asarray(v["sinks_2"])[0], (P, 8)),
            "router": np.asarray(v["o_router"])[0].reshape(KT, P, N_EXPERTS).transpose(1, 0, 2).reshape(P, -1)}
    param = np.concatenate([cols[name] for name in PARAM_COLS], axis=1)
    x = np.concatenate([np.asarray(v["x"]), np.asarray(v["ctx"])], axis=0)
    x = x.reshape(2, T, KT, P).transpose(3, 0, 2, 1).reshape(P, -1)
    ln = [np.broadcast_to(np.asarray(v[n])[0], (P, 512)) for n in ("e_ln_v_g", "e_ln_v_b")]
    w_s = np.asarray(v["e_w_s"])[0].transpose(2, 0, 1).reshape(P, -1)
    b_s = np.repeat(np.asarray(v["e_b_s"])[0].reshape(4, 2, P).transpose(1, 0, 2), 64, axis=0).reshape(P, -1)
    mixer = np.concatenate(ln + [w_s, b_s], axis=1)
    raw = [states(v["b_re_2"][0]), states(v["b_im_2"][0]),
           states(np.asarray(v["c_re_2"])[0].transpose(0, 2, 1)), states(np.asarray(v["c_im_2"])[0].transpose(0, 2, 1))]
    ssm = np.concatenate([a.reshape(P, -1) for a in raw], axis=1)
    return {"const": constants(), "param": param, "x": x, "mixer": mixer, "ssm": ssm}


def kernel(**inputs):
    import concourse.bacc as _bacc
    from concourse.bass_utils import run_bass_kernel_spmd as _run

    nc = _bacc.Bacc("TRN2", target_bir_lowering=False, num_devices=1)
    given = pack(inputs)
    given.update({name: inputs[name] for name in _WEIGHTS})
    arrays, A = {}, {}
    for name, value in given.items():
        a = np.ascontiguousarray(value)
        arrays[f"in_{name}"] = a
        A[name] = nc.dram_tensor(f"in_{name}", a.shape, mybir.dt.from_np(a.dtype), kind="ExternalInput").ap()
    out = nc.dram_tensor("out", (P, KT * T), F32, kind="ExternalOutput").ap()
    build(nc, A, out)
    got = _run(nc, [arrays], core_ids=[0]).results[0]["out"]
    return np.asarray(got).reshape(P, KT, T).transpose(2, 1, 0).reshape(1, T, D)
```
